# Optimizing a Trainium2 kernel written in Bass

```python
import math
import jax, jax.numpy as jnp
from jax import lax
import numpy as np

D_MODEL = 1024
BATCH = 1
SEQ = 256
DEPTH = 1

PLE_DIM = 256
EPS = 1e-6
ROPE_THETA = 10000.0
MOBA_HEADS = 8
MOBA_HEAD_DIM = 64
MOBA_BLOCK = 256
MOBA_TOPK = 3
MOBA_Q_CHUNK = 16
MOBA_WIDTH = MOBA_HEADS * MOBA_HEAD_DIM
MLA_HEADS = 8
MLA_Q_LORA = 256
MLA_KV_LORA = 128
MLA_NOPE_DIM = 64
MLA_ROPE_DIM = 32
MLA_V_DIM = 64
MLA_QK_DIM = MLA_NOPE_DIM + MLA_ROPE_DIM
MLA_WIDTH = MLA_HEADS * MLA_V_DIM
MLA_Q_BLOCK = 128
N_EXPERTS = 32
TOP_K = 4
D_EXPERT = 1024
SWIGLU_LIMIT = 7.0
SWIGLU_ALPHA = 1.702
EXPERT_ROW_BLOCK = 128
IN_SPLITS = (MOBA_WIDTH, MOBA_WIDTH, MOBA_WIDTH, MLA_Q_LORA, MLA_KV_LORA, MLA_ROPE_DIM, D_MODEL, D_MODEL)
D_IN = 3 * MOBA_WIDTH + MLA_Q_LORA + MLA_KV_LORA + MLA_ROPE_DIM + 2 * D_MODEL


def rmsnorm(x, g):
    xf = x.astype(jnp.float32)
    y = xf * lax.rsqrt(jnp.mean(xf * xf, axis=-1, keepdims=True) + EPS)
    return (y * g.astype(jnp.float32)).astype(x.dtype)

def apply_rope(x):
    s, dim = x.shape[-2], x.shape[-1]
    half = dim // 2
    inv_freq = ROPE_THETA ** (-(jnp.arange(half, dtype=jnp.float32) / half))
    ang = jnp.arange(s, dtype=jnp.float32)[:, None] * inv_freq[None, :]
    cos, sin = jnp.cos(ang), jnp.sin(ang)
    xf = x.astype(jnp.float32)
    x1, x2 = xf[..., :half], xf[..., half:]
    return jnp.concatenate([x1 * cos - x2 * sin, x2 * cos + x1 * sin], axis=-1).astype(x.dtype)

def moba_attention(q, k, v):
    b, h, s, hd = q.shape
    nb = -(-s // MOBA_BLOCK)
    s_pad = nb * MOBA_BLOCK
    padcfg = ((0, 0), (0, 0), (0, s_pad - s), (0, 0))
    q, k, v = jnp.pad(q, padcfg), jnp.pad(k, padcfg), jnp.pad(v, padcfg)
    scale = hd ** -0.5
    q_blk = q.reshape(b, h, nb, MOBA_BLOCK, hd)
    k_blk = k.reshape(b, h, nb, MOBA_BLOCK, hd)
    v_blk = v.reshape(b, h, nb, MOBA_BLOCK, hd)
    k_mean = jnp.mean(k_blk.astype(jnp.float32), axis=3)
    gate = jnp.einsum('bhsd,bhnd->bhsn', q.astype(jnp.float32), k_mean)
    cur_blk = jnp.arange(s_pad) // MOBA_BLOCK
    is_past = jnp.arange(nb)[None, :] < cur_blk[:, None]
    gate = jnp.where(is_past, gate, -jnp.inf)
    n_sel = min(MOBA_TOPK, nb)
    _, sel = lax.top_k(gate, n_sel)
    sel_valid = sel < cur_blk[:, None]
    s_own = jnp.einsum('bhnqd,bhnkd->bhnqk', q_blk, k_blk) * scale
    causal = jnp.tril(jnp.ones((MOBA_BLOCK, MOBA_BLOCK), dtype=bool))
    s_own = jnp.where(causal, s_own, -jnp.inf).reshape(b, h, s_pad, MOBA_BLOCK)
    gather_blocks = jax.vmap(jax.vmap(lambda blocks, ix: blocks[ix]))

    def chunk(ci):
        start = ci * MOBA_Q_CHUNK
        qc = lax.dynamic_slice_in_dim(q, start, MOBA_Q_CHUNK, axis=2)
        ix = lax.dynamic_slice_in_dim(sel, start, MOBA_Q_CHUNK, axis=2)
        ok = lax.dynamic_slice_in_dim(sel_valid, start, MOBA_Q_CHUNK, axis=2)
        so = lax.dynamic_slice_in_dim(s_own, start, MOBA_Q_CHUNK, axis=2)
        v_own = lax.dynamic_index_in_dim(v_blk, start // MOBA_BLOCK, axis=2, keepdims=False)
        k_sel = gather_blocks(k_blk, ix)
        v_sel = gather_blocks(v_blk, ix)
        ss = jnp.einsum('bhqd,bhqjkd->bhqjk', qc, k_sel) * scale
        ss = jnp.where(ok[..., None], ss, -jnp.inf)
        logits = jnp.concatenate([so, ss.reshape(b, h, MOBA_Q_CHUNK, n_sel * MOBA_BLOCK)], axis=-1)
        probs = jax.nn.softmax(logits.astype(jnp.float32), axis=-1).astype(v.dtype)
        p_own = probs[..., :MOBA_BLOCK]
        p_sel = probs[..., MOBA_BLOCK:].reshape(b, h, MOBA_Q_CHUNK, n_sel, MOBA_BLOCK)
        return (jnp.einsum('bhqk,bhkd->bhqd', p_own, v_own)
                + jnp.einsum('bhqjk,bhqjkd->bhqd', p_sel, v_sel))

    out = lax.map(chunk, jnp.arange(s_pad // MOBA_Q_CHUNK))
    out = jnp.moveaxis(out, 0, 2).reshape(b, h, s_pad, hd)
    return out[:, :, :s]

def causal_attention(q, k, v):
    b, h, s, dq = q.shape
    scale = dq ** -0.5
    kpos = jnp.arange(s)

    def blk(ci):
        start = ci * MLA_Q_BLOCK
        qc = lax.dynamic_slice_in_dim(q, start, MLA_Q_BLOCK, axis=2)
        sc = jnp.einsum('bhqd,bhkd->bhqk', qc, k).astype(jnp.float32) * scale
        qpos = start + jnp.arange(MLA_Q_BLOCK)
        sc = jnp.where(kpos[None, :] <= qpos[:, None], sc, -jnp.inf)
        pr = jax.nn.softmax(sc, axis=-1).astype(v.dtype)
        return jnp.einsum('bhqk,bhkd->bhqd', pr, v)

    out = lax.map(blk, jnp.arange(s // MLA_Q_BLOCK))
    return jnp.moveaxis(out, 0, 2).reshape(b, h, s, v.shape[-1])

def routed_experts(h, w_router, b_router, w_gate_up, b_gate_up, w_down, b_down):
    b, s, d = h.shape
    n = b * s
    hf = h.reshape(n, d)
    logits = (hf @ w_router).astype(jnp.float32) + b_router.astype(jnp.float32)
    top_vals, top_idx = lax.top_k(logits, TOP_K)
    top_w = jax.nn.softmax(top_vals, axis=-1)
    nk = n * TOP_K
    m = EXPERT_ROW_BLOCK
    flat_e = top_idx.reshape(nk)
    flat_t = jnp.arange(nk, dtype=jnp.int32) // TOP_K
    flat_w = top_w.reshape(nk)
    order = jnp.argsort(flat_e)
    se = flat_e[order]
    counts = jnp.bincount(flat_e, length=N_EXPERTS)
    starts = jnp.cumsum(counts) - counts
    pcounts = ((counts + m - 1) // m) * m
    pends = jnp.cumsum(pcounts)
    pstarts = pends - pcounts
    dest = pstarts[se] + (jnp.arange(nk) - starts[se])
    n_rows = ((nk + m - 1) // m) * m + N_EXPERTS * m
    n_blocks = n_rows // m
    row_tok = jnp.full((n_rows,), n, dtype=jnp.int32).at[dest].set(flat_t[order])
    row_w = jnp.zeros((n_rows,), jnp.float32).at[dest].set(flat_w[order])
    blk_e = jnp.clip(jnp.searchsorted(pends, jnp.arange(n_blocks) * m, side='right'), 0, N_EXPERTS - 1)
    h_pad = jnp.concatenate([hf, jnp.zeros((1, d), hf.dtype)], axis=0)
    xr = h_pad[row_tok].reshape(n_blocks, m, d)

    def expert_block(args):
        xb, e = args
        gu = xb @ w_gate_up[e] + b_gate_up[e]
        g, u = gu[:, :D_EXPERT], gu[:, D_EXPERT:]
        g = jnp.minimum(g, SWIGLU_LIMIT)
        u = jnp.clip(u, -SWIGLU_LIMIT, SWIGLU_LIMIT)
        glu = g * jax.nn.sigmoid(SWIGLU_ALPHA * g)
        return ((u + 1.0) * glu) @ w_down[e] + b_down[e]

    yr = lax.map(expert_block, (xr, blk_e)).reshape(n_rows, d)
    y = jax.ops.segment_sum(yr * row_w[:, None].astype(yr.dtype), row_tok, num_segments=n + 1)[:n]
    return y.reshape(b, s, d).astype(h.dtype)

def hybrid_layer(x, p_i, g_mix, w_in, moba_q_norm, moba_k_norm, mla_q_lat_norm, w_uq,
                 mla_kv_lat_norm, w_ukv, mla_q_norm, mla_k_norm, w_branch_a, w_branch_b, w_out,
                 g_ffn, w_router, b_router, w_gate_up, b_gate_up, w_down, b_down,
                 g_ple, w_ple_gate, w_ple_proj):
    b, s, d = x.shape
    hn = rmsnorm(x, g_mix)
    proj = hn @ w_in
    parts, off = [], 0
    for wdt in IN_SPLITS:
        parts.append(proj[..., off:off + wdt])
        off += wdt
    q_a, k_a, v_a, c_q, c_kv, k_pe, gate_a, gate_b = parts

    heads_a = lambda t: t.reshape(b, s, MOBA_HEADS, MOBA_HEAD_DIM).transpose(0, 2, 1, 3)
    q_a = apply_rope(rmsnorm(heads_a(q_a), moba_q_norm))
    k_a = apply_rope(rmsnorm(heads_a(k_a), moba_k_norm))
    y_a = moba_attention(q_a, k_a, heads_a(v_a))
    y_a = y_a.transpose(0, 2, 1, 3).reshape(b, s, MOBA_WIDTH)

    q_b = (rmsnorm(c_q, mla_q_lat_norm) @ w_uq).reshape(b, s, MLA_HEADS, MLA_QK_DIM).transpose(0, 2, 1, 3)
    kv = (rmsnorm(c_kv, mla_kv_lat_norm) @ w_ukv).reshape(b, s, MLA_HEADS, MLA_NOPE_DIM + MLA_V_DIM).transpose(0, 2, 1, 3)
    k_nope, v_b = kv[..., :MLA_NOPE_DIM], kv[..., MLA_NOPE_DIM:]
    k_pe_h = jnp.broadcast_to(k_pe[:, None], (b, MLA_HEADS, s, MLA_ROPE_DIM))
    k_b = jnp.concatenate([k_nope, k_pe_h], axis=-1)
    q_b = rmsnorm(q_b, mla_q_norm)
    k_b = rmsnorm(k_b, mla_k_norm)
    q_b = jnp.concatenate([q_b[..., :MLA_NOPE_DIM], apply_rope(q_b[..., MLA_NOPE_DIM:])], axis=-1)
    k_b = jnp.concatenate([k_b[..., :MLA_NOPE_DIM], apply_rope(k_b[..., MLA_NOPE_DIM:])], axis=-1)
    y_b = causal_attention(q_b, k_b, v_b)
    y_b = y_b.transpose(0, 2, 1, 3).reshape(b, s, MLA_WIDTH)

    merged = jax.nn.sigmoid(gate_a) * (y_a @ w_branch_a) + jax.nn.sigmoid(gate_b) * (y_b @ w_branch_b)
    x = x + merged @ w_out

    x = x + routed_experts(rmsnorm(x, g_ffn), w_router, b_router, w_gate_up, b_gate_up, w_down, b_down)

    hp = rmsnorm(x, g_ple)
    x = x + jax.nn.sigmoid(hp @ w_ple_gate) * (p_i @ w_ple_proj)
    return x

def first_inputs(seed: int = 0) -> dict:
    key = jax.random.key(seed)
    ks = jax.random.split(key, 32)
    f32 = jnp.float32

    def nrm(k, shape, scale):
        return jax.random.normal(k, shape, f32) * scale

    def gain(k, dim):
        return 1.0 + 0.02 * jax.random.normal(k, (DEPTH, dim), f32)

    L = DEPTH
    return {
        "x": nrm(ks[0], (BATCH, SEQ, D_MODEL), 1.0),
        "p": nrm(ks[1], (DEPTH, BATCH, SEQ, PLE_DIM), 1.0),
        "g_mix": gain(ks[2], D_MODEL),
        "w_in": nrm(ks[3], (L, D_MODEL, D_IN), D_MODEL ** -0.5),
        "moba_q_norm": gain(ks[4], MOBA_HEAD_DIM),
        "moba_k_norm": gain(ks[5], MOBA_HEAD_DIM),
        "mla_q_lat_norm": gain(ks[6], MLA_Q_LORA),
        "w_uq": nrm(ks[7], (L, MLA_Q_LORA, MLA_HEADS * MLA_QK_DIM), MLA_Q_LORA ** -0.5),
        "mla_kv_lat_norm": gain(ks[8], MLA_KV_LORA),
        "w_ukv": nrm(ks[9], (L, MLA_KV_LORA, MLA_HEADS * (MLA_NOPE_DIM + MLA_V_DIM)), MLA_KV_LORA ** -0.5),
        "mla_q_norm": gain(ks[10], MLA_QK_DIM),
        "mla_k_norm": gain(ks[11], MLA_QK_DIM),
        "w_branch_a": nrm(ks[12], (L, MOBA_WIDTH, D_MODEL), MOBA_WIDTH ** -0.5),
        "w_branch_b": nrm(ks[13], (L, MLA_WIDTH, D_MODEL), MLA_WIDTH ** -0.5),
        "w_out": nrm(ks[14], (L, D_MODEL, D_MODEL), D_MODEL ** -0.5),
        "g_ffn": gain(ks[15], D_MODEL),
        "w_router": nrm(ks[16], (L, D_MODEL, N_EXPERTS), D_MODEL ** -0.5),
        "b_router": nrm(ks[17], (L, N_EXPERTS), 0.01),
        "w_gate_up": nrm(ks[18], (L, N_EXPERTS, D_MODEL, 2 * D_EXPERT), D_MODEL ** -0.5),
        "b_gate_up": nrm(ks[19], (L, N_EXPERTS, 2 * D_EXPERT), 0.01),
        "w_down": nrm(ks[20], (L, N_EXPERTS, D_EXPERT, D_MODEL), D_EXPERT ** -0.5),
        "b_down": nrm(ks[21], (L, N_EXPERTS, D_MODEL), 0.01),
        "g_ple": gain(ks[22], D_MODEL),
        "w_ple_gate": nrm(ks[23], (L, D_MODEL, D_MODEL), D_MODEL ** -0.5),
        "w_ple_proj": nrm(ks[24], (L, PLE_DIM, D_MODEL), PLE_DIM ** -0.5),
    }

def first_block(x, p, g_mix, w_in, moba_q_norm, moba_k_norm, mla_q_lat_norm, w_uq,
              mla_kv_lat_norm, w_ukv, mla_q_norm, mla_k_norm, w_branch_a, w_branch_b, w_out,
              g_ffn, w_router, b_router, w_gate_up, b_gate_up, w_down, b_down,
              g_ple, w_ple_gate, w_ple_proj):
    for i in range(DEPTH):
        x = hybrid_layer(x, p[i], g_mix[i], w_in[i], moba_q_norm[i], moba_k_norm[i],
                         mla_q_lat_norm[i], w_uq[i], mla_kv_lat_norm[i], w_ukv[i],
                         mla_q_norm[i], mla_k_norm[i], w_branch_a[i], w_branch_b[i], w_out[i],
                         g_ffn[i], w_router[i], b_router[i], w_gate_up[i], b_gate_up[i],
                         w_down[i], b_down[i], g_ple[i], w_ple_gate[i], w_ple_proj[i])
    return x


DEPTH_2 = 2

CONV_WIDTH = D_MODEL // 2
CONV_HEADS = 8
CONV_K = 3
POOL_WIDTH = D_MODEL // 2
POOL_WINDOWS = (2, 4, 8, 16)
POOL_GROUPS = len(POOL_WINDOWS)
POOL_GROUP_DIM = POOL_WIDTH // POOL_GROUPS
MIX_WIDTH = CONV_WIDTH + POOL_WIDTH
IN_COLS = 4 * CONV_WIDTH + 2 * POOL_WIDTH
NORM_EPS = 1e-6


def rms_norm(x, g):
    xf = x.astype(jnp.float32)
    y = xf * lax.rsqrt(jnp.mean(xf * xf, axis=-1, keepdims=True) + NORM_EPS)
    return (y * g.astype(jnp.float32)).astype(x.dtype)

def causal_depthwise_conv(z, w):
    C = z.shape[-1]
    return lax.conv_general_dilated(
        z, w[:, None, :].astype(z.dtype),
        window_strides=(1,), padding=[(CONV_K - 1, 0)],
        dimension_numbers=("NWC", "WIO", "NWC"),
        feature_group_count=C)

def causal_multiscale_pool(p, w_pool, pool_scale):
    B, T, _ = p.shape
    pf = p.astype(jnp.float32)
    pos = jnp.arange(1, T + 1, dtype=jnp.float32)[None, :, None]
    outs = []
    for g, w in enumerate(POOL_WINDOWS):
        pg = pf[..., g * POOL_GROUP_DIM:(g + 1) * POOL_GROUP_DIM]
        s = jnp.cumsum(pg, axis=1)
        lag = jnp.pad(s, ((0, 0), (w, 0), (0, 0)))[:, :T]
        mean = (s - lag) / jnp.minimum(pos, float(w))
        outs.append(mean - pg)
    pooled = jnp.stack(outs, axis=2).astype(p.dtype)
    mixed = jnp.einsum("btgc,gcd->btgd", pooled, w_pool)
    return mixed.reshape(B, T, POOL_WIDTH) * pool_scale

def second_inputs(seed: int = 0) -> dict:
    key = jax.random.key(seed)
    ks = jax.random.split(key, 12)
    f32 = jnp.float32
    x = jax.random.normal(ks[0], (BATCH, SEQ, D_MODEL), f32)
    c = jax.random.normal(ks[1], (BATCH, D_MODEL), f32)
    w_ada = jax.random.normal(ks[2], (DEPTH_2, D_MODEL, 3 * D_MODEL), f32) * D_MODEL ** -0.5
    b_ada = 0.01 * jax.random.normal(ks[3], (DEPTH_2, 3 * D_MODEL), f32)
    g_pre = 1.0 + 0.02 * jax.random.normal(ks[4], (DEPTH_2, D_MODEL), f32)
    w_in = jax.random.normal(ks[5], (DEPTH_2, D_MODEL, IN_COLS), f32) * D_MODEL ** -0.5
    w_conv = jax.random.normal(ks[6], (DEPTH_2, CONV_K, CONV_WIDTH), f32) * CONV_K ** -0.5
    w_pool = jax.random.normal(ks[7], (DEPTH_2, POOL_GROUPS, POOL_GROUP_DIM, POOL_GROUP_DIM), f32) * POOL_GROUP_DIM ** -0.5
    pool_scale = 1.0 + 0.1 * jax.random.normal(ks[8], (DEPTH_2, POOL_WIDTH), f32)
    w_out = jax.random.normal(ks[9], (DEPTH_2, MIX_WIDTH, D_MODEL), f32) * MIX_WIDTH ** -0.5
    g_post = 1.0 + 0.02 * jax.random.normal(ks[10], (DEPTH_2, D_MODEL), f32)
    return {"x": x, "c": c, "w_ada": w_ada, "b_ada": b_ada, "g_pre": g_pre, "w_in": w_in,
            "w_conv": w_conv, "w_pool": w_pool, "pool_scale": pool_scale,
            "w_out": w_out, "g_post": g_post}

def second_block(x, c, w_ada, b_ada, g_pre, w_in, w_conv, w_pool, pool_scale, w_out, g_post):
    B, T, D = x.shape
    c_act = jax.nn.silu(c)
    cw = CONV_WIDTH
    for l in range(DEPTH_2):
        mod = c_act @ w_ada[l] + b_ada[l]
        shift, scale, gate = jnp.split(mod, 3, axis=-1)
        h = rms_norm(x, g_pre[l]) * (1.0 + scale[:, None, :]) + shift[:, None, :]
        proj = h @ w_in[l]
        u_a = proj[..., 0 * cw:1 * cw]
        b_a = proj[..., 1 * cw:2 * cw]
        c_a = proj[..., 2 * cw:3 * cw]
        gate_a = proj[..., 3 * cw:4 * cw]
        o = 4 * cw
        u_p = proj[..., o:o + POOL_WIDTH]
        gate_p = proj[..., o + POOL_WIDTH:o + 2 * POOL_WIDTH]
        y_a = b_a * causal_depthwise_conv(c_a * u_a, w_conv[l]) * jax.nn.silu(gate_a)
        y_p = causal_multiscale_pool(u_p, w_pool[l], pool_scale[l]) * jax.nn.silu(gate_p)
        y = jnp.concatenate([y_a, y_p], axis=-1) @ w_out[l]
        x = x + gate[:, None, :] * rms_norm(y, g_post[l])
    return x


def setup_inputs(seed=0):
    out = dict(first_inputs(seed))
    for name, value in second_inputs(seed + 1).items():
        if name != "x":
            out[name + "_2"] = value
    return out


def reference(
    x, p, g_mix, w_in, moba_q_norm, moba_k_norm, mla_q_lat_norm, w_uq, mla_kv_lat_norm, w_ukv,
    mla_q_norm, mla_k_norm, w_branch_a, w_branch_b, w_out, g_ffn, w_router, b_router, w_gate_up,
    b_gate_up, w_down, b_down, g_ple, w_ple_gate, w_ple_proj, c_2, w_ada_2, b_ada_2, g_pre_2,
    w_in_2, w_conv_2, w_pool_2, pool_scale_2, w_out_2, g_post_2,
):
    x = first_block(
        x, p, g_mix, w_in, moba_q_norm, moba_k_norm, mla_q_lat_norm, w_uq, mla_kv_lat_norm,
        w_ukv, mla_q_norm, mla_k_norm, w_branch_a, w_branch_b, w_out, g_ffn, w_router, b_router,
        w_gate_up, b_gate_up, w_down, b_down, g_ple, w_ple_gate, w_ple_proj,
    )
    return second_block(
        x, c_2, w_ada_2, b_ada_2, g_pre_2, w_in_2, w_conv_2, w_pool_2, pool_scale_2, w_out_2,
        g_post_2,
    )


_drawn_inputs = setup_inputs


def setup_inputs(seed=0):
    import zlib

    import numpy as np

    out = dict(_drawn_inputs(seed))
    spreads = {}
    factors = {'moba_q_norm': 3.107,
     'moba_k_norm': 3.696,
     'mla_q_lat_norm': 6.933,
     'mla_kv_lat_norm': 4.156,
     'mla_q_norm': 2.918,
     'mla_k_norm': 4.051,
     'b_gate_up': 7.992,
     'b_down': 8.0,
     'g_ple': 39.664,
     'b_ada_2': 3.136,
     'g_post_2': 4.135}
    for name, (base, spread) in spreads.items():
        noise = np.random.default_rng([zlib.crc32(name.encode()), seed]).standard_normal(out[name].shape)
        drawn = base * np.exp(spread * noise) if base else spread * noise
        out[name] = __import__('jax').numpy.asarray(drawn.astype(out[name].dtype))
    for name, factor in factors.items():
        out[name] = (out[name] * factor).astype(out[name].dtype)
    return out
```

```python
import numpy as np
import concourse.bass as bass
from concourse import mybir
from contextlib import ExitStack

P = 128
S, D = 256, 1024
HALVES = S // P
KC = D // P
HEADS, HD = 8, 64
QL, KVL, ROPE, QK = 256, 128, 32, 96
NOPE, VD = 64, 64
E, TOPK, F = 32, 4, 1024
CAP = 64
ROUNDS = S // CAP
PCOLS = ROUNDS * E
EPS = 1e-6
LIMIT, ALPHA = 7.0, 1.702
THETA = 10000.0
LAYERS = 2
NEG = -1e30
POOL_WINDOWS = (2, 4, 8, 16)
PAD = 16
SLOTS = 12
SLOT = 2048

C_ID, C_BEFORE, C_ONES, C_SLOT = 0, P, 2 * P, 3 * P
C_CAUSAL = 4 * P
C_MCOS = C_CAUSAL + 3 * P
C_MSIN = C_MCOS + HALVES * HD
C_LCOS = C_MSIN + HALVES * HD
C_LSIN = C_LCOS + HALVES * ROPE
C_SEL = C_LSIN + HALVES * ROPE
C_THR = C_SEL + PCOLS
C_MHALF = C_THR + ROUNDS
NCONST = C_MHALF + 1

A_MIX, A_LAT, A_FFN, A_PLE = 0, 8, 11, 19
A_PRE, A_POST, A_CONV, A_PSC = 27, 43, 59, 83
NA = 91
B_ADA, B_C = 0, 48
NB = 56


def shape_constants():
    c = np.zeros((P, NCONST), np.float32)
    c[:, C_ID:C_ID + P] = np.eye(P)
    c[:, C_BEFORE:C_BEFORE + P] = np.triu(np.ones((P, P)), 1)
    c[:, C_ONES:C_ONES + P] = 1.0
    c[:, C_SLOT:C_SLOT + P] = np.tile(np.arange(CAP), 2)
    above = np.where(np.tril(np.ones((P, P))) > 0, 0.0, NEG)
    c[:, C_CAUSAL:C_CAUSAL + P] = above
    c[:, C_CAUSAL + 2 * P:C_CAUSAL + 3 * P] = above

    def rope(dim):
        half = dim // 2
        inv = np.float32(THETA) ** (-(np.arange(half, dtype=np.float32) / np.float32(half)))
        ang = np.arange(S, dtype=np.float32)[:, None] * inv[None, :].astype(np.float32)
        cos, sin = np.cos(ang), np.sin(ang)
        put = lambda a: a.reshape(HALVES, P, dim).transpose(1, 0, 2).reshape(P, HALVES * dim)
        return put(np.concatenate([cos, cos], 1)), put(np.concatenate([-sin, sin], 1))

    c[:, C_MCOS:C_MSIN], c[:, C_MSIN:C_LCOS] = rope(HD)
    c[:, C_LCOS:C_LSIN], c[:, C_LSIN:C_SEL] = rope(ROPE)
    for k in range(E):
        c[k, C_SEL + k:C_SEL + PCOLS:E] = 1.0
    c[:, C_THR:C_THR + ROUNDS] = (np.arange(ROUNDS) + 1) * CAP
    c[:, C_MHALF] = -0.5
    inv = np.stack([1.0 / np.minimum(np.arange(1, S + 1), w) for w in POOL_WINDOWS]).astype(np.float32)
    return c, np.ascontiguousarray(np.broadcast_to(inv.reshape(1, -1), (P, 4 * S)))


def build(nc, t, out):
    fp32, i32, u32 = mybir.dt.float32, mybir.dt.int32, mybir.dt.uint32
    ALU = mybir.AluOpType
    ACT = mybir.ActivationFunctionType
    AX = mybir.AxisListType.X
    V, G, A, T = nc.vector, nc.gpsimd, nc.scalar, nc.tensor
    ds = bass.ds

    ctx = ExitStack()
    with ctx:
        def sb(name, shape, dt=fp32):
            return ctx.enter_context(nc.sbuf_tensor(name, shape, dt))

        def sem(name):
            return ctx.enter_context(nc.semaphore(name))

        ring = sb("ring", [P, SLOTS, SLOT])
        X = sb("X", [P, HALVES, D])
        HN = sb("HN", [P, HALVES, D])
        HT = sb("HT", [P, KC, S])
        const = sb("const", [P, NCONST])
        arena = sb("arena", [P, 72 * 256])
        tabs = sb("tabs", [P, 4 * HALVES * HD + 4 * HALVES * ROPE])
        gains = sb("gains", [P, 2 * HD + 2 * QK + E])
        colA = sb("colA", [P, NA])
        colB = sb("colB", [P, NB])
        mods = sb("mods", [P, LAYERS, 24])
        wr = sb("wr", [P, KC, E])
        posm = sb("posm", [P, HALVES, PCOLS + 1])
        wtok = sb("wtok", [P, HALVES, PCOLS])
        st = sb("st", [P, 128])
        nextra = sb("nextra", [P, 1], i32)
        top_i = sb("top_i", [P, HALVES, 8], u32)
        ps = ctx.enter_context(nc.psum_tensor("ps", [P, 8, 512], fp32))

        def view(kb, n, pattern=None, **kw):
            a = arena[:, kb * 256:kb * 256 + n]
            return a.rearrange(pattern, **kw) if pattern else a

        ident = const[:, C_ID:C_ID + P]
        before = const[:, C_BEFORE:C_BEFORE + P]
        ones = const[:, C_ONES:C_ONES + P]
        slots = const[:, C_SLOT:C_SLOT + P]
        causal = const[:, C_CAUSAL:C_CAUSAL + 3 * P]

        hn_flat = HN[:].rearrange("p a b -> p (a b)")
        acc = [view(0, 3 * D), view(12, 3 * D)]
        acc_halves = view(0, 6 * D, "p (l h n) -> p l h n", l=LAYERS, h=2)
        gate = [view(0, HALVES * D, "p (a b) -> p a b", a=HALVES), view(24, HALVES * D, "p (a b) -> p a b", a=HALVES)]
        wukv = view(8, D)
        qTb = view(8, HEADS * S, "p (a b) -> p a b", a=HEADS)
        kTb = view(16, HEADS * S, "p (a b) -> p a b", a=HEADS)
        latn = view(16, HALVES * 416, "p (a b) -> p a b", a=HALVES)
        latT = view(20, 3 * S, "p (a b) -> p a b", a=3)
        mT = view(8, KC * S, "p (a b) -> p a b", a=KC)
        moba = [view(24 + 4 * i, HALVES * 512, "p (a b) -> p a b", a=HALVES) for i in range(3)]
        qTa = hn_flat[:, 0:D].rearrange("p (a b) -> p a b", a=4)
        kTa = hn_flat[:, D:2 * D].rearrange("p (a b) -> p a b", a=4)
        ada_ring = view(36, 2 * 1536, "p (a b) -> p a b", a=2)
        qm = view(36, HALVES * HEADS * QK, "p (a b) -> p a b", a=HALVES)
        km = view(42, HALVES * HEADS * QK, "p (a b) -> p a b", a=HALVES)
        wuq = view(48, 2 * 768, "p (a b) -> p a b", a=2)
        kv = view(48, HALVES * D, "p (a b) -> p a b", a=HALVES)
        merged = kv
        SQ = view(56, HALVES * 768)
        vec_rows = view(56, 2 * P, "p (a b) -> p a b", a=2)
        SW = view(62, 1024)
        lat = view(66, HALVES * 416, "p (a b) -> p a b", a=HALVES)
        prob = view(66, 2 * 384, "p (a b) -> p a b", a=2)
        probT = view(69, 2 * 384, "p (a b) -> p a b", a=2)
        lg, mask, ex, em, pm = [SQ[:, 64 * i:64 * i + 64].rearrange("p (a b) -> p a b", a=HALVES) for i in range(5)]
        top_v = SQ[:, 320:336].rearrange("p (a b) -> p a b", a=HALVES)
        top_f = SQ[:, 336:352].rearrange("p (a b) -> p a b", a=HALVES)

        xg = view(0, KC * CAP, "p (a b) -> p a b", a=KC)
        glu, sig, upc, hid, hidT = [view(2 + 2 * i, 512) for i in range(5)]
        bias = view(12, 3 * D)
        yslot = view(24, 512)
        scat = view(26, HALVES * P, "p (a b) -> p a b", a=HALVES)
        pick = view(27, HALVES * CAP, "p (a b) -> p a b", a=HALVES)
        pickw = view(28, HALVES * P, "p (a b) -> p a b", a=HALVES)
        esel = view(29, CAP)

        wo2 = view(0, KC * D, "p (a b) -> p a b", a=KC)
        W3 = PAD + S
        U = view(32, 4 * W3, "p (a b) -> p a b", a=4)
        WA = arena[:, 36 * 256 + 64:36 * 256 + 64 + 4 * W3].rearrange("p (a b) -> p a b", a=4)
        WB = arena[:, 40 * 256 + 128:40 * 256 + 128 + 4 * W3].rearrange("p (a b) -> p a b", a=4)
        diag, conv = WB[:, :, PAD:W3], WA[:, :, PAD:W3]
        PL, SG, T1, UA = [view(45 + 4 * i, D) for i in range(4)]
        Z = arena[:, 61 * 256:61 * 256 + 4 * (S + 2)].rearrange("p (a b) -> p a b", a=4)
        invw = arena[:, 65 * 256 + 32:65 * 256 + 32 + D]
        wpool = arena[:, 69 * 256 + 64:69 * 256 + 64 + 512].rearrange("p (a b) -> p a b", a=4)
        pin = view(45, HALVES * 256, "p (a b) -> p a b", a=HALVES)
        pT = view(47, 2 * S, "p (a b) -> p a b", a=2)
        yT3 = hn_flat.rearrange("p (a b) -> p a b", a=KC)

        TM = HALVES * HD
        mtab = [[tabs[:, (2 * i + j) * TM:(2 * i + j + 1) * TM] for j in range(2)] for i in range(2)]
        o = 4 * TM
        LT = HALVES * ROPE
        ltab = []
        for i in range(2):
            ltab.append([tabs[:, o + j * LT:o + (j + 1) * LT] for j in range(2)])
            o += 2 * LT
        g_mq, g_mk = gains[:, 0:HD], gains[:, HD:2 * HD]
        g_lq, g_lk = gains[:, 2 * HD:2 * HD + QK], gains[:, 2 * HD + QK:2 * HD + 2 * QK]
        b_rt = gains[:, 2 * HD + 2 * QK:2 * HD + 2 * QK + E]

        names = """x_in const_in vec_in gain_in wuq_in wukv_in wr_in bias_in p_in inv_in wpool_in wo2_in
        out_stored dve_step act_step pow_in pow_out tables_done
        x_sums hn_done c_sigmoid ada_summed q_ready k_ready lat_ready mlaq_ready mlak_ready
        s_full s_free scored prob_done t_full t_free pv_done y_done
        gates_open merged_done ffn_sums hn2_done lg_ready mask_done expd routed
        used_ada0 used_ada1 full_ada0 full_ada1 chunk_used1 chunk_used2 chunk_used3
        pick_ready pickw_ready esel_ready xg_ready gather_done gu_ready gu_used
        g_ready mid_ready sig_ready hid_ready scatT_done scat_ready hidT_full hidT_ready
        down_done y_ready sc_ready sc_used
        pads_set ple_sums hn3_done ple_sig x_ready
        l_sums l_hn l_pooled l_gp_sig l_gp_used l_gpz l_ga_sig l_conv l_diag l_ysum l_tmp l_step""".split()
        s = {n: sem(n) for n in names}
        ring1 = [sem(f"ring1_{i}") for i in range(SLOTS)]
        ring2 = [sem(f"ring2_{i}") for i in range(SLOTS)]
        ring3 = [sem(f"ring3_{i}") for i in range(SLOTS)]
        full1, moved1 = [sem(f"full1_{p}") for p in range(4)], [sem(f"moved1_{p}") for p in range(4)]
        full3, moved3 = [sem(f"full3_{p}") for p in range(4)], [sem(f"moved3_{p}") for p in range(4)]
        fullL, movedL = [sem(f"fullL_{p}") for p in range(4)], [sem(f"movedL_{p}") for p in range(4)]

        FIRST = 1

        def ordinals(uses):
            fills, moves, at = [0] * 4, [0] * 4, {}
            for name, p, chunks in uses:
                at[name] = (p, fills[p], moves[p], chunks)
                moves[p] += 1
                fills[p] += chunks is None
            return at, fills, moves
        N = None
        U1, _, _ = ordinals([("vec", 3, N), ("hT0", 0, N), ("hT1", 1, N), ("q", 2, 2), ("k", 3, 4), ("lat", 0, 6),
                             ("v", 1, 8), ("ga0", 2, 10), ("ada", 3, N), ("ga1", 1, 12), ("latT", 0, N),
                             ("qTa", 3, N), ("kTa", 2, N), ("qm0", 0, N), ("qm1", 1, N), ("kv0", 3, N),
                             ("kv1", 2, N), ("gb0", 2, 14), ("gb1", 2, 16), ("qTb0", 2, N), ("qTb1", 0, N),
                             ("kTb0", 1, N), ("kTb1", 2, N), ("yTa", 2, N), ("yTb", 0, N),
                             ("A0", 1, 17), ("B0", 2, 18), ("A1", 3, 19), ("B1", 0, 20),
                             ("mT0", 1, N), ("mT1", 2, N), ("o0", 3, 22), ("o1", 0, 24),
                             ("fT0", 1, N), ("fT1", 2, N), ("rt", 3, N), ("pos", 0, N)])
        U3, _, _ = ordinals([("hT0", 0, N), ("hT1", 1, N), ("pT", 2, N), ("pp0", 3, 1), ("pp1", 0, 1),
                             ("g0", 1, 3), ("g1", 2, 5)])
        UL, LF, LM = ordinals([("hT0", 0, N), ("hT1", 1, N), ("up", 2, 2), ("gp", 3, 4), ("ua", 0, 6), ("mix", 1, N),
                               ("ca", 2, 8), ("ba", 3, 10), ("ga", 0, 12), ("gpb", 1, N), ("y0", 2, N), ("y1", 3, N)])

        def filled(eng, name):
            p, fills, _, chunks = U1[name]
            if chunks:
                eng.wait_ge(s["chunk_used1"], chunks)
            else:
                eng.wait_ge(full1[p], fills + 1)
            return p

        def moved(eng, name):
            eng.wait_ge(moved1[U1[name][0]], U1[name][2] + 1)
            return U1[name][0]

        def free(pe, name):
            if U1[name][2]:
                pe.wait_ge(moved1[U1[name][0]], U1[name][2])
            return U1[name][0]

        def filled3(eng, name):
            p, fills, _, chunks = U3[name]
            if chunks:
                eng.wait_ge(s["chunk_used3"], chunks)
            else:
                eng.wait_ge(full3[p], fills + 1)
            return p

        def moved3_(eng, name):
            eng.wait_ge(moved3[U3[name][0]], U3[name][2] + 1)
            return U3[name][0]

        def filledL(eng, l, name):
            p, fills, _, chunks = UL[name]
            if chunks:
                eng.wait_ge(s["chunk_used3"], l * SLOTS + (PRE3 + chunks))
            else:
                eng.wait_ge(fullL[p], l * LF[p] + (fills + 1))
            return p

        def movedL_(eng, l, name):
            p, _, moves, _ = UL[name]
            eng.wait_ge(movedL[p], l * LM[p] + (moves + 1 + FIRST))
            return p

        def pair(p):
            return ps[:, 2 * p:2 * p + 2, :]

        def flat(p, n=1024, at=0):
            return ps[:, 2 * p:2 * p + 2, :].rearrange("p a b -> p (a b)")[:, at:at + n]

        def cols(a, i, l=None):
            return a[:, i:i + 1] if l is None else a[:, ds(l + i, 1)]

        mods_f = mods[:].rearrange("p a b -> p (a b)")

        def k_rows(w, r0, nk, c0, n):
            return w[0, r0:r0 + nk * P, c0:c0 + n].rearrange("(k p) n -> p k n", p=P)

        col_groups = [(0, 512), (512, 512), (1536, 416), (1024, 512),
                      (1952, 512), (2464, 512), (2976, 512), (3488, 512)]
        GROUP1 = ["q", "k", "lat", "v", "ga0", "ga1", "gb0", "gb1"]
        LSTEPS = 22
        chunks1 = []
        for c0, n in col_groups:
            for kh in range(2):
                chunks1.append((k_rows(t["w_in"], kh * 512, 4, c0, n), 4, n))
        for g in range(2):
            for w in (t["w_branch_a"], t["w_branch_b"]):
                chunks1.append((k_rows(w, 0, 4, g * 512, 512), 4, 512))
        for g in range(2):
            for kh in range(2):
                chunks1.append((k_rows(t["w_out"], kh * 512, 4, g * 512, 512), 4, 512))
        N1 = len(chunks1)
        assert N1 == 2 * SLOTS

        chunks3 = [(k_rows(t["w_ple_proj"], 0, 2, 0, D), 2, D)]
        for g in range(2):
            for kh in range(2):
                chunks3.append((k_rows(t["w_ple_gate"], kh * 512, 4, g * 512, 512), 4, 512))
        PRE3 = len(chunks3)
        GROUPL = [("up", 4), ("gp", 5), ("ua", 0), ("ca", 2), ("ba", 1), ("ga", 3)]
        assert 2 * len(GROUPL) == SLOTS
        for l in range(LAYERS):
            for _, g in GROUPL:
                for kh in range(2):
                    chunks3.append((t["w_in_2"][l, kh * 512:kh * 512 + 512, g * 512:g * 512 + 512]
                                    .rearrange("(k p) n -> p k n", p=P), 4, 512))

        def slot(i, a, b):
            return ring[:, i % SLOTS, 0:a * b].rearrange("p (a b) -> p a b", a=a)

        ada_v = t["w_ada_2"].rearrange("l (k p) n -> (l k) p n", p=P)
        gu_v = t["w_gate_up"].rearrange("a e (k p) n -> (a e) k p n", p=P)
        dn_v = t["w_down"].rearrange("a e (j k p) n -> (a e) j p k n", p=P, k=2)

        block = ctx.enter_context(nc.Block())

        @block.sync
        def _(sp):
            for n, (src, a, b) in enumerate(chunks1):
                if n >= SLOTS:
                    sp.wait_ge(s["chunk_used1"], n - SLOTS + 1)
                sp.dma_start(slot(n, a, b), src).then_inc(ring1[n % SLOTS], 16)

            def expert(e, used):
                for j in range(SLOTS):
                    used(j)
                    if j < KC:
                        src = gu_v[ds(e, 1), j].rearrange("e p n -> (e p) n")
                        sp.dma_start(ring[:, j, :], src).then_inc(ring2[j], 16)
                    else:
                        src = dn_v[ds(e, 1), j - KC].rearrange("e p k n -> (e p) k n")
                        sp.dma_start(slot(j, 2, D), src).then_inc(ring2[j], 16)

            expert(0, lambda j: sp.wait_ge(s["chunk_used1"], N1 - SLOTS + j + 1))
            with sp.Fori(0, E - 1) as before_e:
                expert(before_e + 1, lambda j: sp.wait_ge(s["chunk_used2"], before_e * SLOTS + (j + 1)))
            sp.wait_ge(s["routed"], 1)
            extra = sp.value_load(nextra[0:1, 0:1], min_val=0, max_val=ROUNDS - 1)
            with sp.If(extra > 0):
                with sp.Fori(0, extra) as r:
                    with sp.Fori(0, E) as e:
                        expert(e, lambda j: sp.wait_ge(s["chunk_used2"],
                                                       r * (E * SLOTS) + e * SLOTS + ((E - 1) * SLOTS + j + 1)))
            for n, (src, a, b) in enumerate(chunks3):
                if n < SLOTS:
                    sp.wait_ge(s["chunk_used2"], extra * (E * SLOTS) + ((E - 1) * SLOTS + n + 1))
                else:
                    sp.wait_ge(s["chunk_used3"], n - SLOTS + 1)
                sp.dma_start(slot(n, a, b), src).then_inc(ring3[n % SLOTS], 16)
                if n == SLOTS:
                    sp.wait_ge(s["hn3_done"], 2)
                    sp.dma_start(wo2, t["w_out_2"][0].rearrange("(k p) n -> p k n", p=P)).then_inc(s["wo2_in"], 16)
            sp.wait_ge(s["x_ready"], 2)
            sp.dma_start(wo2, t["w_out_2"][1].rearrange("(k p) n -> p k n", p=P)).then_inc(s["wo2_in"], 16)
            sp.wait_ge(s["x_ready"], 1 + LAYERS)
            sp.dma_start(out[0].rearrange("(h p) n -> p h n", p=P), X[:]).then_inc(s["out_stored"], 16)
            sp.wait_ge(s["out_stored"], 16)

        @block.gpsimd
        def _(pool):
            for hf in range(2):
                G.memset(acc_halves[:, :, hf, :], 0.0).then_inc(s[f"used_ada{hf}"], FIRST)
            for a in [s[n] for n in ("down_done", "scatT_done", "gu_used", "sc_used")] + movedL:
                pool.sem_inc(a, FIRST)
            pool.wait_ge(s["const_in"], 16)
            pool.wait_ge(s["gain_in"], 16 * 5)

            def b2(a, w):
                return a.unsqueeze(1).to_broadcast([P, HALVES, w])

            def hv(a):
                return a.rearrange("p (h w) -> p h w", h=HALVES)

            def table(dst, cos, sin, g, w):
                G.tensor_tensor(hv(dst[0]), hv(cos), b2(g, w), ALU.mult)
                h = w // 2
                G.tensor_tensor(hv(dst[1])[:, :, 0:h], hv(sin)[:, :, 0:h], b2(g[:, h:w], h), ALU.mult)
                return G.tensor_tensor(hv(dst[1])[:, :, h:w], hv(sin)[:, :, h:w], b2(g[:, 0:h], h), ALU.mult)
            for i, g in ((0, g_mq), (1, g_mk)):
                table(mtab[i], const[:, C_MCOS:C_MSIN], const[:, C_MSIN:C_LCOS], g, HD)
            for i, g in ((0, g_lq), (1, g_lk)):
                last = table(ltab[i], const[:, C_LCOS:C_LSIN], const[:, C_LSIN:C_SEL], g[:, NOPE:QK], ROPE)
            last.then_inc(s["tables_done"], 1)

            powers = [0]

            def power(w0, n):
                powers[0] += 1
                pool.wait_ge(s["pow_in"], powers[0])
                G.tensor_tensor(st[:, w0:w0 + n], st[:, w0:w0 + n],
                                const[:, C_MHALF:C_MHALF + 1].to_broadcast([P, n]),
                                ALU.pow).then_inc(s["pow_out"], 1)

            def ada(layer):
                with pool.Fori(layer * KC, layer * KC + KC) as i:
                    for hf in range(2):
                        pool.wait_ge(s[f"used_ada{hf}"], i + FIRST)
                        pool.dma_start(ada_ring[:, hf, :],
                                       ada_v[ds(i, 1), :, hf * 1536:hf * 1536 + 1536].rearrange("l p n -> (l p) n")
                                       ).then_inc(s[f"full_ada{hf}"], 16)

            power(0, 2)
            ada(0)
            ada(1)
            power(16, 16)
            power(32, 16)
            filled(pool, "ada")
            pool.dma_start(wukv, t["w_ukv"][0]).then_inc(s["wukv_in"], 16)
            power(0, 4)
            power(16, 16)
            power(32, 16)
            pool.wait_ge(s["chunk_used1"], N1)
            pool.dma_start(bias[0:E, 0:2 * F], t["b_gate_up"][0]).then_inc(s["bias_in"], 16)
            pool.dma_start(bias[0:E, 2 * F:2 * F + D], t["b_down"][0]).then_inc(s["bias_in"], 16)
            power(0, 2)
            pool.wait_ge(s["routed"], 1)
            pool.dma_start(pin, t["p"][0, 0].rearrange("(h p) n -> p h n", p=P)).then_inc(s["p_in"], 16)
            pool.dma_start(invw, t["inv_windows"]).then_inc(s["inv_in"], 16)
            for z, n in ((U, PAD), (WA, PAD), (WB, PAD), (Z, 2)):
                G.memset(z[:, :, 0:n], 0.0).then_inc(s["pads_set"], 1)
            power(0, 2)
            with pool.Fori(0, LAYERS) as l:
                pool.wait_ge(movedL[1], l * LM[1] + FIRST)
                pool.dma_start(wpool, t["w_pool_2"][ds(l, 1)].rearrange("l g c d -> c (l g) d")
                               ).then_inc(s["wpool_in"], 16)
                for i in range(2):
                    pool.wait_ge(s["pow_in"], l * 2 + (powers[0] + i + 1))
                    G.tensor_tensor(st[:, 0:2], st[:, 0:2], const[:, C_MHALF:C_MHALF + 1].to_broadcast([P, 2]),
                                    ALU.pow).then_inc(s["pow_out"], 1)

        @block.scalar
        def _(act):
            act.dma_start(X[:], t["x"][0].rearrange("(h p) n -> p h n", p=P)).then_inc(s["x_in"], 16)
            act.dma_start(const[:], t["consts"]).then_inc(s["const_in"], 16)
            rows = [(t["g_mix"].rearrange("a (k n) -> (a k) n", n=P), 0, A_MIX),
                    (t["mla_q_lat_norm"].rearrange("a (k n) -> (a k) n", n=P), 0, A_LAT),
                    (t["mla_kv_lat_norm"].rearrange("a (k n) -> (a k) n", n=P), 0, A_LAT + 2),
                    (t["g_ffn"].rearrange("a (k n) -> (a k) n", n=P), 0, A_FFN),
                    (t["g_ple"].rearrange("a (k n) -> (a k) n", n=P), 0, A_PLE),
                    (t["g_pre_2"].rearrange("a (k n) -> (a k) n", n=P), 0, A_PRE),
                    (t["g_post_2"].rearrange("a (k n) -> (a k) n", n=P), 0, A_POST),
                    (t["w_conv_2"].rearrange("l k (c n) -> (l k c) n", n=P), 0, A_CONV),
                    (t["pool_scale_2"].rearrange("l (c n) -> (l c) n", n=P), 0, A_PSC),
                    (t["b_ada_2"].rearrange("l (c n) -> (l c) n", n=P), 1, B_ADA),
                    (t["c_2"].rearrange("a (k n) -> (a k) n", n=P), 1, B_C)]
            for src, i, r in rows:
                act.dma_start(vec_rows[r:r + src.shape[0], i, :], src).then_inc(s["vec_in"], 16)
            for dst, src in ((g_mq, t["moba_q_norm"]), (g_mk, t["moba_k_norm"]), (g_lq, t["mla_q_norm"]),
                             (g_lk, t["mla_k_norm"]), (b_rt, t["b_router"])):
                act.dma_start(dst, src[0].partition_broadcast(P)).then_inc(s["gain_in"], 16)
            act.dma_start(wuq, t["w_uq"][0].rearrange("(k p) n -> p k n", p=P)).then_inc(s["wuq_in"], 16)
            act.dma_start(wr[:], t["w_router"][0].rearrange("(k p) n -> p k n", p=P)).then_inc(s["wr_in"], 16)

            act.wait_ge(s["x_in"], 16)
            for h in range(HALVES):
                A.activation(HN[:, h, :], X[:, h, :], ACT.Square, accum_out=st[:, h:h + 1]).then_inc(s["x_sums"], 1)
            p = filled(act, "vec")
            A.copy(colA[:], ps[:, 2 * p, 0:NA])
            A.copy(colB[:], ps[:, 2 * p + 1, 0:NB]).then_inc(moved1[p], 1)
            act.wait_ge(moved1[p], 1)
            A.activation(st[:, 100:108], colB[:, B_C:B_C + KC], ACT.Sigmoid).then_inc(s["c_sigmoid"], 1)

            def scaled(p, done, dst, n, gain):
                for i in range(n):
                    last = A.activation(dst(i), flat(p, S, i * S), ACT.Copy, scale=gain(i))
                last.then_inc(done[p], 1)

            for j in range(2):
                scaled(filled(act, f"hT{j}"), moved1, lambda i: HT[:, 4 * j + i, :], 4,
                       lambda i: cols(colA, A_MIX + 4 * j + i))

            def move(name, dst, src):
                p = filled(act, name)
                A.copy(dst, src(p)).then_inc(moved1[p], 1)

            move("q", moba[0], pair)
            move("k", moba[1], pair)
            move("lat", lat, lambda p: pair(p)[:, :, 0:416])
            move("v", moba[2], pair)
            filled(act, "ada")
            for g in range(2):
                move(f"ga{g}", gate[0][:, :, g * 512:g * 512 + 512], pair)
            scaled(filled(act, "latT"), moved1, lambda i: latT[:, i, :], 3, lambda i: cols(colA, A_LAT + i))
            for h in range(HALVES):
                move(f"qm{h}", qm[:, h, :], lambda p: flat(p, 768))
            for h in range(HALVES):
                move(f"kv{h}", kv[:, h, :], flat)
            for h in range(2 * HEADS):
                b, scale = h % 2, (HD if h < HEADS else QK) ** -0.5
                act.wait_ge(s["scored"], h + 1)
                c = 64 + h // HEADS * 16 + h % HEADS
                A.activation(prob[:, b, 0:P], prob[:, b, 0:P], ACT.Exp, bias=st[:, 48 + 2 * b:49 + 2 * b],
                             scale=scale, accum_out=st[:, c:c + 1])
                A.activation(prob[:, b, P:3 * P], prob[:, b, P:3 * P], ACT.Exp, bias=st[:, 49 + 2 * b:50 + 2 * b],
                             scale=scale, accum_out=st[:, c + 8:c + 9]).then_inc(s["prob_done"], 1)
                if h in (3, 7):
                    move(f"gb{h // 4}", gate[1][:, :, h // 4 * 512:h // 4 * 512 + 512], pair)
                if h == HEADS - 1:
                    for dst, tag in ((qTb, "qTb"), (kTb, "kTb")):
                        for j in range(2):
                            move(f"{tag}{j}", dst[0:QK, 4 * j:4 * j + 4, :],
                                 lambda p: flat(p)[0:QK].rearrange("p (a b) -> p a b", a=4))
            move("yTa", HT[:, 0:4, :].rearrange("p a b -> p (a b)"), flat)
            move("yTb", HT[:, 4:8, :].rearrange("p a b -> p (a b)"), flat)
            for i in range(2):
                A.activation(gate[i], gate[i], ACT.Sigmoid).then_inc(s["gates_open"], 1)
            for j in range(2):
                move(f"mT{j}", mT[:, 4 * j:4 * j + 4, :].rearrange("p a b -> p (a b)"), flat)
            moved(act, "o0")
            moved(act, "o1")
            for h in range(HALVES):
                A.activation(HN[:, h, :], X[:, h, :], ACT.Square, accum_out=st[:, h:h + 1]).then_inc(s["ffn_sums"], 1)
            for j in range(2):
                scaled(filled(act, f"fT{j}"), moved1, lambda i: HT[:, 4 * j + i, :], 4,
                       lambda i: cols(colA, A_FFN + 4 * j + i))
            act.wait_ge(s["lg_ready"], 1)
            for h in range(HALVES):
                A.activation(ex[:, h, :], lg[:, h, :], ACT.Exp, bias=st[:, 4 + h:5 + h]).then_inc(s["expd"], 1)

            act.wait_ge(s["routed"], 1)
            extra = act.value_load(nextra[0:1, 0:1], min_val=0, max_val=ROUNDS - 1)
            with act.Fori(0, extra * E + E) as i:
                act.wait_ge(s["g_ready"], i + 1)
                A.activation(sig, glu, ACT.Sigmoid, scale=ALPHA).then_inc(s["sig_ready"], 1)
                act.wait_ge(s["scatT_done"], i + (1 + FIRST))
                act.wait_ge(s["sc_ready"], i * 2 + 2)
                A.copy(scat, ps[:, 4, 0:HALVES * P].rearrange("p (a b) -> p a b", a=HALVES)
                       ).then_inc(s["scat_ready"], 1)
                act.wait_ge(s["hidT_full"], i + 1)
                A.copy(hidT, ps[:, 3, :]).then_inc(s["hidT_ready"], 1)
                act.wait_ge(s["down_done"], i + (1 + FIRST))
                A.copy(yslot, ps[:, 5, :]).then_inc(s["y_ready"], 1)

            act.wait_ge(s["sc_used"], extra * (2 * E) + (2 * E + 2 + FIRST))
            for h in range(HALVES):
                A.activation(HN[:, h, :], X[:, h, :], ACT.Square, accum_out=st[:, h:h + 1]).then_inc(s["ple_sums"], 1)
            p = filled3(act, "pT")
            A.copy(pT, flat(p, 512).rearrange("p (a b) -> p a b", a=2)).then_inc(moved3[p], 1)
            for j in range(2):
                scaled(filled3(act, f"hT{j}"), moved3, lambda i: HT[:, 4 * j + i, :], 4,
                       lambda i: cols(colA, A_PLE + 4 * j + i))
            for g in range(2):
                p = filled3(act, f"g{g}")
                if g:
                    act.wait_ge(s["l_tmp"], 1)
                A.activation(SG.rearrange("p (a b) -> p a b", a=HALVES), pair(p), ACT.Sigmoid).then_inc(moved3[p], 1)

            with act.Fori(0, LAYERS) as l:
                act.wait_ge(s["x_ready"], l + 1)
                for h in range(HALVES):
                    A.activation(HN[:, h, :], X[:, h, :], ACT.Square,
                                 accum_out=st[:, h:h + 1]).then_inc(s["l_sums"], 1)
                p = filledL(act, l, "hT0")
                for k in range(4):
                    last = A.activation(HT[:, k, :], flat(p, S, k * S), ACT.Identity,
                                        bias=cols(mods_f, k, l * 24), scale=cols(mods_f, 8 + k, l * 24))
                last.then_inc(movedL[p], 1)
                p = filledL(act, l, "up")
                act.wait_ge(s["pads_set"], 4)
                A.copy(U[:, :, PAD:W3], flat(p).rearrange("p (a b) -> p a b", a=4)).then_inc(movedL[p], 1)
                p = filledL(act, l, "gp")
                A.activation(SG, flat(p), ACT.Sigmoid).then_inc(s["l_gp_sig"], 1)
                p = filledL(act, l, "ua")
                A.copy(UA, flat(p)).then_inc(movedL[p], 1)
                p = filledL(act, l, "ga")
                movedL_(act, l, "gp")
                A.activation(SG, flat(p), ACT.Sigmoid).then_inc(s["l_ga_sig"], 1)
                p = filledL(act, l, "gpb")
                movedL_(act, l, "ca")
                A.copy(UA, flat(p)).then_inc(movedL[p], 1)
                act.wait_ge(s["l_conv"], l + 1)
                for g in range(2):
                    p = filledL(act, l, f"y{g}")
                    for h in range(HALVES):
                        if g:
                            act.wait_ge(s["l_ysum"], l * 4 + (h + 1))
                        A.activation(SG[:, h * 512:h * 512 + 512], ps[:, 2 * p + h, :], ACT.Square,
                                     accum_out=st[:, 8 + 2 * h + g:9 + 2 * h + g]).then_inc(s["l_ysum"], 1)

        @block.vector
        def _(dve):
            steps = [0]

            def run(ins):
                steps[0] += 1
                ins.then_inc(s["dve_step"], 1)

            def join():
                dve.wait_ge(s["dve_step"], steps[0])

            powers = [0]

            def power():
                powers[0] += 1
                dve.wait_ge(s["pow_out"], powers[0])

            dve.wait_ge(s["x_sums"], 2)
            V.tensor_scalar(st[:, 0:2], st[:, 0:2], 1.0 / D, EPS, ALU.mult, ALU.add).then_inc(s["pow_in"], 1)
            power()
            for h in range(HALVES):
                V.tensor_scalar(HN[:, h, :], X[:, h, :], st[:, h:h + 1], None, ALU.mult).then_inc(s["hn_done"], 1)
            dve.wait_ge(s["c_sigmoid"], 1)
            cact = st[:, 108:116]
            run(V.tensor_tensor(cact, st[:, 100:108], colB[:, B_C:B_C + KC], ALU.mult))
            join()

            def ada(layer):
                with dve.Fori(0, KC) as k:
                    for hf in range(2):
                        a = acc[layer][:, hf * 1536:hf * 1536 + 1536]
                        n = layer * KC
                        dve.wait_ge(s[f"full_ada{hf}"], k * 16 + (n + 1) * 16)
                        dve.wait_ge(s[f"used_ada{hf}"], k + (n + FIRST))
                        V.scalar_tensor_tensor(a, ada_ring[:, hf, :], cact[:, ds(k, 1)], a, ALU.mult,
                                               ALU.add).then_inc(s[f"used_ada{hf}"], 1)

            def mod_columns():
                p = filled(dve, "ada")
                V.tensor_tensor(mods_f, ps[:, 2 * p, 0:24 * LAYERS], colB[:, B_ADA:B_ADA + 24 * LAYERS],
                                ALU.add).then_inc(moved1[p], 1)
                moved(dve, "ada")
                for l in range(LAYERS):
                    m = mods[:, l, :]
                    run(V.scalar_tensor_tensor(m[:, 8:16], m[:, 8:16], 1.0, colA[:, A_PRE + 8 * l:A_PRE + 8 * l + 8],
                                               ALU.add, ALU.mult))
                    run(V.tensor_tensor(m[:, 16:24], m[:, 16:24], colA[:, A_POST + 8 * l:A_POST + 8 * l + 8],
                                        ALU.mult))
                join()

            def mean_squares(x, w, n0):
                xs = x.rearrange("p a (h d) -> p (a h) d", d=w)
                sq = SQ[:, 0:HALVES * HEADS * w].rearrange("p (a d) -> p a d", d=w)
                run(V.tensor_tensor(sq, xs, xs, ALU.mult))
                join()
                run(V.tensor_reduce(st[:, n0:n0 + 16], sq, AX, ALU.add))
                join()
                V.tensor_scalar(st[:, n0:n0 + 16], st[:, n0:n0 + 16], 1.0 / w, EPS, ALU.mult,
                                ALU.add).then_inc(s["pow_in"], 1)

            def unit_heads(x, w, n0):
                power()
                xs = x.rearrange("p a (h d) -> p (a h) d", d=w)
                run(V.tensor_tensor(xs, xs, st[:, n0:n0 + 16].unsqueeze(2).to_broadcast([P, 16, w]), ALU.mult))
                join()

            def rope(x, tab, w, done):
                h = w // 2
                sw = SW[:, 0:HALVES * HEADS * w].rearrange("p (a h d) -> p a h d", a=HALVES, h=HEADS)
                tb = [a.rearrange("p (a d) -> p a d", a=HALVES).unsqueeze(2) for a in tab]
                run(V.tensor_tensor(sw[:, :, :, 0:h], x[:, :, :, h:w],
                                    tb[1][:, :, :, 0:h].to_broadcast([P, HALVES, HEADS, h]), ALU.mult))
                run(V.tensor_tensor(sw[:, :, :, h:w], x[:, :, :, 0:h],
                                    tb[1][:, :, :, h:w].to_broadcast([P, HALVES, HEADS, h]), ALU.mult))
                join()
                run(V.tensor_tensor(x, x, tb[0].to_broadcast([P, HALVES, HEADS, w]), ALU.mult))
                join()
                V.tensor_tensor(x, x, sw, ALU.add).then_inc(s[done], 1)
                dve.wait_ge(s[done], 1)

            def four(x, d):
                return x.rearrange("p a (h d) -> p a h d", d=d)

            ada(0)
            ada(1)
            dve.wait_ge(s["tables_done"], 1)
            for i, (raw, done) in enumerate((("q", "q_ready"), ("k", "k_ready"))):
                moved(dve, raw)
                mean_squares(moba[i], HD, 16 + 16 * i)
                unit_heads(moba[i], HD, 16 + 16 * i)
                rope(four(moba[i], HD), mtab[i], HD, done)
            moved(dve, "lat")
            sq = SQ[:, 0:HALVES * 384].rearrange("p (a b) -> p a b", a=HALVES)
            run(V.tensor_tensor(sq, lat[:, :, 0:384], lat[:, :, 0:384], ALU.mult))
            join()
            run(V.tensor_reduce(st[:, 0:2], sq[:, :, 0:QL], AX, ALU.add))
            run(V.tensor_reduce(st[:, 2:4], sq[:, :, QL:384], AX, ALU.add))
            join()
            run(V.tensor_scalar(st[:, 0:2], st[:, 0:2], 1.0 / QL, EPS, ALU.mult, ALU.add))
            V.tensor_scalar(st[:, 2:4], st[:, 2:4], 1.0 / KVL, EPS, ALU.mult, ALU.add).then_inc(s["pow_in"], 1)
            mod_columns()
            power()
            run(V.tensor_copy(latn[:, :, 384:416], lat[:, :, 384:416]))
            run(V.tensor_tensor(latn[:, :, 0:QL], lat[:, :, 0:QL],
                                st[:, 0:2].unsqueeze(2).to_broadcast([P, HALVES, QL]), ALU.mult))
            V.tensor_tensor(latn[:, :, QL:384], lat[:, :, QL:384],
                            st[:, 2:4].unsqueeze(2).to_broadcast([P, HALVES, KVL]), ALU.mult
                            ).then_inc(s["lat_ready"], 1)
            for name, dst in (("qTa", qTa), ("kTa", kTa)):
                p = filled(dve, name)
                V.tensor_copy(dst, flat(p).rearrange("p (a b) -> p a b", a=4)).then_inc(moved1[p], 1)

            def mla_step(i):
                x, tag, g = ((qm, "mlaq_ready", g_lq), (km, "mlak_ready", g_lk))[i // 3]
                if i == 0:
                    moved(dve, "qm0")
                    moved(dve, "qm1")
                if i == 3:
                    moved(dve, "kv0")
                    moved(dve, "kv1")
                    kvh = kv.rearrange("p a (h d) -> p (a h) d", d=NOPE + VD)
                    run(V.tensor_copy(km.rearrange("p a (h d) -> p (a h) d", d=QK)[:, :, 0:NOPE], kvh[:, :, 0:NOPE]))
                    run(V.tensor_copy(four(km, QK)[:, :, :, NOPE:QK],
                                      latn[:, :, 384:416].unsqueeze(2).to_broadcast([P, HALVES, HEADS, ROPE])))
                    join()
                if i % 3 == 0:
                    mean_squares(x, QK, 16 + 16 * (i // 3))
                elif i % 3 == 1:
                    unit_heads(x, QK, 16 + 16 * (i // 3))
                else:
                    xs = x.rearrange("p a (h d) -> p (a h) d", d=QK)
                    run(V.tensor_tensor(xs[:, :, 0:NOPE], xs[:, :, 0:NOPE],
                                        g[:, 0:NOPE].unsqueeze(1).to_broadcast([P, 16, NOPE]), ALU.mult))
                    rope(four(x, QK)[:, :, :, NOPE:QK], ltab[i // 3], ROPE, tag)

            def score(h):
                b, scale = h % 2, (HD if h < HEADS else QK) ** -0.5
                bank = 2 * b
                dve.wait_ge(s["s_full"], h + 1)
                if h >= 2:
                    dve.wait_ge(s["t_full"], h - 1)
                run(V.tensor_tensor_reduce(out=prob[:, b, 0:P], in0=ps[:, bank, 0:P], in1=causal[:, 0:P], scale=1.0,
                                           scalar=-3e38, op0=ALU.add, op1=ALU.max,
                                           accum_out=st[:, 48 + 2 * b:49 + 2 * b]))
                V.tensor_tensor_reduce(out=prob[:, b, P:3 * P], in0=ps[:, bank, P:3 * P], in1=causal[:, P:3 * P],
                                       scale=1.0, scalar=-3e38, op0=ALU.add, op1=ALU.max,
                                       accum_out=st[:, 49 + 2 * b:50 + 2 * b]).then_inc(s["s_free"], 1)
                dve.wait_ge(s["s_free"], h + 1)
                join()
                V.tensor_scalar(st[:, 48 + 2 * b:50 + 2 * b], st[:, 48 + 2 * b:50 + 2 * b], -scale, None,
                                ALU.mult).then_inc(s["scored"], 1)

            def out_of_t(h):
                dve.wait_ge(s["t_full"], h + 1)
                if h >= 2:
                    dve.wait_ge(s["pv_done"], h - 1)
                V.tensor_copy(probT[:, h % 2, :], ps[:, 2 * (h % 2) + 1, 0:3 * P]).then_inc(s["t_free"], 1)

            def normalise(br):
                dve.wait_ge(s["pv_done"], HEADS * (br + 1))
                r = st[:, 64 + 16 * br:80 + 16 * br]
                run(V.reciprocal(r, r))
                join()
                V.tensor_tensor(HN[:, br, :].rearrange("p (a d) -> p a d", d=HD),
                                flat(3).rearrange("p (a d) -> p a d", d=HD),
                                r.unsqueeze(2).to_broadcast([P, 16, HD]), ALU.mult).then_inc(s["y_done"], 1)

            for h0 in (0, HEADS):
                for h in range(h0, h0 + HEADS + 1):
                    if h < h0 + HEADS:
                        score(h)
                    if h > h0:
                        out_of_t(h - 1)
                    if h0 == 0 and h < 6:
                        mla_step(h)
                normalise(h0 // HEADS)

            dve.wait_ge(s["gates_open"], 2)
            tmp = SQ[:, 0:HALVES * 512].rearrange("p (a b) -> p a b", a=HALVES)
            for g in range(2):
                part = slice(g * 512, g * 512 + 512)
                p = filled(dve, f"A{g}")
                V.tensor_tensor(merged[:, :, part], gate[0][:, :, part], pair(p), ALU.mult).then_inc(moved1[p], 1)
                moved(dve, f"A{g}")
                p = filled(dve, f"B{g}")
                V.tensor_tensor(tmp, gate[1][:, :, part], pair(p), ALU.mult).then_inc(moved1[p], 1)
                moved(dve, f"B{g}")
                V.tensor_tensor(merged[:, :, part], merged[:, :, part], tmp, ALU.add).then_inc(s["merged_done"], 1)
                dve.wait_ge(s["merged_done"], g + 1)
            for g in range(2):
                p = filled(dve, f"o{g}")
                part = X[:, :, g * 512:g * 512 + 512]
                V.tensor_tensor(part, part, pair(p), ALU.add).then_inc(moved1[p], 1)
            dve.wait_ge(s["ffn_sums"], 2)
            V.tensor_scalar(st[:, 0:2], st[:, 0:2], 1.0 / D, EPS, ALU.mult, ALU.add).then_inc(s["pow_in"], 1)
            power()
            for h in range(HALVES):
                V.tensor_scalar(HN[:, h, :], X[:, h, :], st[:, h:h + 1], None, ALU.mult).then_inc(s["hn2_done"], 1)

            p = filled(dve, "rt")
            V.tensor_tensor(lg, ps[:, 2 * p, 0:HALVES * E].rearrange("p (a b) -> p a b", a=HALVES),
                            b_rt.unsqueeze(1).to_broadcast([P, HALVES, E]), ALU.add).then_inc(moved1[p], 1)
            moved(dve, "rt")
            for h in range(HALVES):
                run(V.max(top_v[:, h, :], lg[:, h, :]))
            join()
            for h in range(HALVES):
                run(V.max_index(top_i[:, h, :], top_v[:, h, :], lg[:, h, :]))
            V.tensor_scalar(st[:, 4:6], top_v[:, :, 0], -1.0, None, ALU.mult).then_inc(s["lg_ready"], 1)
            join()
            run(V.tensor_copy(top_f, top_i[:]))
            join()
            for j in range(TOPK):
                for h in range(HALVES):
                    idx = top_f[:, h, j:j + 1]
                    if j == 0:
                        ins = V.tensor_scalar(mask[:, h, :], slots[:, 0:E], idx, None, ALU.is_equal)
                    else:
                        ins = V.scalar_tensor_tensor(mask[:, h, :], slots[:, 0:E], idx, mask[:, h, :],
                                                     ALU.is_equal, ALU.add)
                    if j < TOPK - 1:
                        run(ins)
                    else:
                        ins.then_inc(s["mask_done"], 1)
                join()
            dve.wait_ge(s["mask_done"], 2)
            dve.wait_ge(s["expd"], 2)
            run(V.tensor_tensor(em, ex, mask, ALU.mult))
            join()
            run(V.tensor_reduce(st[:, 6:8], em, AX, ALU.add))
            join()
            run(V.reciprocal(st[:, 6:8], st[:, 6:8]))
            join()
            for h in range(HALVES):
                run(V.tensor_scalar(wtok[:, h, :].rearrange("p (r e) -> p r e", e=E),
                                    em[:, h, :].unsqueeze(1).to_broadcast([P, ROUNDS, E]), st[:, 6 + h:7 + h], None,
                                    ALU.mult))
            p = filled(dve, "pos")
            pos = ps[:, 2 * p, 0:HALVES * E].rearrange("p (a b) -> p a b", a=HALVES)
            run(V.scalar_tensor_tensor(pm, pos, 1.0, mask, ALU.add, ALU.mult))
            run(V.tensor_reduce(st[:, 8:9], ps[:, 2 * p, 2 * E:3 * E], AX, ALU.max))
            run(V.memset(posm[:, :, PCOLS:PCOLS + 1], -1.0))
            V.memset(yslot, 0.0).then_inc(s["y_ready"], 1)
            join()
            for r in range(ROUNDS):
                run(V.tensor_scalar(posm[:, :, r * E:r * E + E], pm, -1.0 - CAP * r, None, ALU.add))
            run(V.tensor_scalar(st[:, 12:12 + ROUNDS], const[:, C_THR:C_THR + ROUNDS], st[:, 8:9], None, ALU.is_lt))
            join()
            run(V.tensor_reduce(st[:, 9:10], st[:, 12:12 + ROUNDS], AX, ALU.add))
            join()
            V.tensor_copy(nextra[:], st[:, 9:10]).then_inc(s["routed"], 1)
            V.memset(scat, 0.0).then_inc(s["scat_ready"], 1)
            dve.wait_ge(s["routed"], 1)

            def pick_tokens(c, inc):
                for h in range(HALVES):
                    last = V.tensor_scalar(pick[:, h, :], slots[:, 0:CAP], posm[:, h, ds(c, 1)], None, ALU.is_equal)
                last.then_inc(s["pick_ready"], 1)

            def gathered():
                return V.tensor_tensor(xg, ps[:, 2, :].rearrange("p (a b) -> p a b", a=KC),
                                       colA[:, A_FFN:A_FFN + KC].unsqueeze(2).to_broadcast([P, KC, CAP]), ALU.mult)

            pick_tokens(0, 1)
            dve.wait_ge(s["gather_done"], 1)
            gathered().then_inc(s["xg_ready"], 1)
            extra = dve.value_load(nextra[0:1, 0:1], min_val=0, max_val=ROUNDS - 1)

            def add_scattered(n, h):
                dve.wait_ge(s["sc_ready"], n + 1)
                dve.wait_ge(s["sc_used"], n + FIRST)
                V.tensor_tensor(X[:, h, :], X[:, h, :], flat(3), ALU.add).then_inc(s["sc_used"], 1)

            with dve.Fori(0, extra * E + E) as i:
                dve.wait_ge(s["down_done"], i + FIRST)
                V.tensor_copy(esel[0:E, :], const[0:E, ds(i + C_SEL, 1)].to_broadcast([E, CAP])
                              ).then_inc(s["esel_ready"], 1)
                dve.wait_ge(s["scatT_done"], i + FIRST)
                for h in range(HALVES):
                    last = V.tensor_scalar(pickw[:, h, :], slots, posm[:, h, ds(i, 1)], wtok[:, h, ds(i, 1)],
                                           ALU.is_equal, ALU.mult)
                last.then_inc(s["pickw_ready"], 1)
                dve.wait_ge(s["gather_done"], i + 1)
                pick_tokens(i + 1, 1)
                for h in range(HALVES):
                    add_scattered(i * 2 + h, h)
                dve.wait_ge(s["gu_ready"], i + 1)
                V.tensor_scalar(glu, ps[:, 0, :], LIMIT, None, ALU.min).then_inc(s["g_ready"], 1)
                V.tensor_scalar(upc, ps[:, 1, :], LIMIT, -LIMIT, ALU.min, ALU.max).then_inc(s["gu_used"], 1)
                dve.wait_ge(s["g_ready"], i + 1)
                dve.wait_ge(s["gu_used"], i + (1 + FIRST))
                V.scalar_tensor_tensor(upc, upc, 1.0, glu, ALU.add, ALU.mult).then_inc(s["mid_ready"], 1)
                dve.wait_ge(s["mid_ready"], i + 1)
                dve.wait_ge(s["sig_ready"], i + 1)
                V.tensor_tensor(hid, upc, sig, ALU.mult).then_inc(s["hid_ready"], 1)
                dve.wait_ge(s["gather_done"], i + 2)
                gathered().then_inc(s["xg_ready"], 1)
            for h in range(HALVES):
                add_scattered(extra * (2 * E) + (2 * E + h), h)

            dve.wait_ge(s["ple_sums"], 2)
            V.tensor_scalar(st[:, 0:2], st[:, 0:2], 1.0 / D, EPS, ALU.mult, ALU.add).then_inc(s["pow_in"], 1)
            power()
            for h in range(HALVES):
                V.tensor_scalar(HN[:, h, :], X[:, h, :], st[:, h:h + 1], None, ALU.mult).then_inc(s["hn3_done"], 1)
            T1h = T1.rearrange("p (a b) -> p a b", a=HALVES)
            for g in range(2):
                moved3_(dve, f"g{g}")
                p = filled3(dve, f"pp{g}")
                V.tensor_tensor(T1h, SG.rearrange("p (a b) -> p a b", a=HALVES), pair(p), ALU.mult
                                ).then_inc(s["l_tmp"], 1)
                dve.wait_ge(s["l_tmp"], g + 1)
                part = X[:, :, g * 512:g * 512 + 512]
                ins = V.tensor_tensor(part, part, T1h, ALU.add)
                if g:
                    ins.then_inc(s["x_ready"], 1)
                else:
                    run(ins)
                    join()
            P0 = powers[0]

            with dve.Fori(0, LAYERS) as l:
                nl = [0]

                def lrun(ins):
                    nl[0] += 1
                    ins.then_inc(s["l_step"], 1)

                def ljoin():
                    dve.wait_ge(s["l_step"], l * LSTEPS + nl[0])

                def lfilled(name):
                    return filledL(dve, l, name)

                def lmoved(name):
                    return movedL_(dve, l, name)

                dve.wait_ge(s["l_sums"], l * 2 + 2)
                V.tensor_scalar(st[:, 0:2], st[:, 0:2], 1.0 / D, EPS, ALU.mult, ALU.add).then_inc(s["pow_in"], 1)
                dve.wait_ge(s["pow_out"], l * 2 + (P0 + 1))
                for h in range(HALVES):
                    V.tensor_scalar(HN[:, h, :], X[:, h, :], st[:, h:h + 1], None, ALU.mult).then_inc(s["l_hn"], 1)
                p = lfilled("hT1")
                for k in range(4):
                    last = V.tensor_scalar(HT[:, 4 + k, :], flat(p, S, k * S), cols(mods_f, 12 + k, l * 24),
                                           cols(mods_f, 4 + k, l * 24), ALU.mult, ALU.add)
                last.then_inc(movedL[p], 1)
                lmoved("up")
                dve.wait_ge(s["pads_set"], 4)

                def shifted(a, g0, by):
                    return a[:, g0:4, PAD - by:W3 - by]
                for dst, src, g0, by in ((WA, U, 0, 1), (WB, WA, 1, 2), (WA, WB, 2, 4), (WB, WA, 3, 8)):
                    lrun(V.tensor_tensor(shifted(dst, g0, 0), shifted(src, g0, 0), shifted(src, g0, by), ALU.add))
                    ljoin()
                pl4 = PL.rearrange("p (a b) -> p a b", a=4)
                iv4 = invw.rearrange("p (a b) -> p a b", a=4)
                dve.wait_ge(s["inv_in"], 16)
                for g in range(4):
                    lrun(V.tensor_tensor(pl4[:, g, :], (WA if g % 2 == 0 else WB)[:, g, PAD:W3], iv4[:, g, :], ALU.mult))
                ljoin()
                V.tensor_tensor(pl4, pl4, U[:, :, PAD:W3], ALU.subtract).then_inc(s["l_pooled"], 1)
                gp = mods_f[:, ds(l * 24 + 16, KC)].rearrange("p (a b) -> p a b", b=2)
                V.tensor_tensor(diag.rearrange("p a (b c) -> p a b c", b=2),
                                ident.unsqueeze(1).unsqueeze(1).to_broadcast([P, 4, 2, P]),
                                gp.unsqueeze(3).to_broadcast([P, 4, 2, P]), ALU.mult).then_inc(s["l_diag"], 1)
                p = lfilled("gp")
                dve.wait_ge(s["l_gp_sig"], l + 1)
                V.tensor_tensor(T1, SG, flat(p), ALU.mult).then_inc(movedL[p], 1)
                lmoved("gp")
                p = lfilled("mix")
                for g in range(4):
                    last = V.scalar_tensor_tensor(yT3[:, 4 + g, :], flat(p, S, g * S), cols(colA, A_PSC + g, l * 4),
                                                  T1[:, g * S:g * S + S], ALU.mult, ALU.mult)
                last.then_inc(movedL[p], 1)
                lmoved("ua")
                p = lfilled("ca")
                V.tensor_tensor(Z[:, :, 2:S + 2], flat(p).rearrange("p (a b) -> p a b", a=4),
                                UA.rearrange("p (a b) -> p a b", a=4), ALU.mult).then_inc(movedL[p], 1)
                lmoved("ca")
                for k in (2, 1, 0):
                    for c in range(4):
                        w = cols(colA, A_CONV + k * 4 + c, l * 12)
                        z = Z[:, c, k:k + S]
                        if k == 2:
                            lrun(V.tensor_scalar(conv[:, c, :], z, w, None, ALU.mult))
                        else:
                            lrun(V.scalar_tensor_tensor(conv[:, c, :], z, w, conv[:, c, :], ALU.mult, ALU.add))
                    ljoin()
                p = lfilled("ba")
                V.tensor_tensor(conv, conv, flat(p).rearrange("p (a b) -> p a b", a=4), ALU.mult
                                ).then_inc(movedL[p], 1)
                lmoved("ba")
                p = lfilled("ga")
                dve.wait_ge(s["l_ga_sig"], l + 1)
                lmoved("mix")
                V.tensor_tensor(T1, SG, flat(p), ALU.mult).then_inc(movedL[p], 1)
                lmoved("ga")
                V.tensor_tensor(yT3[:, 0:4, :], conv, T1.rearrange("p (a b) -> p a b", a=4), ALU.mult
                                ).then_inc(s["l_conv"], 1)
                dve.wait_ge(s["l_conv"], l + 1)
                dve.wait_ge(s["l_ysum"], l * 4 + 4)
                lrun(V.tensor_reduce(st[:, 0:2], st[:, 8:12].rearrange("p (a b) -> p a b", a=2), AX, ALU.add))
                ljoin()
                V.tensor_scalar(st[:, 0:2], st[:, 0:2], 1.0 / D, EPS, ALU.mult, ALU.add).then_inc(s["pow_in"], 1)
                dve.wait_ge(s["pow_out"], l * 2 + (P0 + 2))
                lmoved("gpb")
                T1h = T1.rearrange("p (a b) -> p a b", a=HALVES)
                for g in range(2):
                    p = UL[f"y{g}"][0]
                    for h in range(HALVES):
                        ins = V.scalar_tensor_tensor(T1h[:, h, :], ps[:, 2 * p + h, :], st[:, h:h + 1],
                                                     UA[:, g * 512:g * 512 + 512], ALU.mult, ALU.mult)
                        if h:
                            ins.then_inc(movedL[p], 1)
                    lmoved(f"y{g}")
                    part = X[:, :, g * 512:g * 512 + 512]
                    ins = V.tensor_tensor(part, part, T1h, ALU.add)
                    if g:
                        ins.then_inc(s["x_ready"], 1)
                    else:
                        lrun(ins)
                        ljoin()
                assert nl[0] == LSTEPS

        @block.tensor
        def _(pe):
            def chunk(n):
                pe.wait_ge(ring1[n % SLOTS], 16 * (n // SLOTS + 1))

            def features(p, src, n=4, w=P):
                for k in range(n):
                    for h in range(HALVES):
                        last = T.transpose(flat(p, P, k * S + h * P)[0:w], src(k, h), ident)
                return last

            pe.wait_ge(s["const_in"], 16)
            pe.wait_ge(s["vec_in"], 16 * 11)
            p = free(pe, "vec")
            T.transpose(ps[:, 2 * p, 0:NA], vec_rows[0:NA, 0, :], ident[0:NA, 0:NA])
            T.transpose(ps[:, 2 * p + 1, 0:NB], vec_rows[0:NB, 1, :], ident[0:NB, 0:NB]).then_inc(full1[p], 1)
            pe.wait_ge(s["hn_done"], 2)
            for j in range(2):
                p = free(pe, f"hT{j}")
                features(p, lambda k, h: HN[:, h, (4 * j + k) * P:(4 * j + k + 1) * P]).then_inc(full1[p], 1)

            def project(gi, kh, halves=(0, 1)):
                name, n, c = GROUP1[gi], col_groups[gi][1], 2 * gi + kh
                chunk(c)
                moved(pe, f"hT{kh}")
                p = free(pe, name)
                for h in halves:
                    for k in range(4):
                        last = T.matmul(ps[:, 2 * p + h, 0:n], HT[:, 4 * kh + k, h * P:h * P + P],
                                        slot(c, 4, n)[:, k, :], start=kh + k == 0, stop=4 * kh + k == KC - 1)
                if halves[-1]:
                    last.then_inc(s["chunk_used1"], 1)

            for gi in range(5):
                for kh in range(2):
                    project(gi, kh)
            p = free(pe, "ada")
            for hf in range(2):
                pe.wait_ge(s[f"used_ada{hf}"], LAYERS * KC + FIRST)
            for c in range(24 * LAYERS):
                last = T.matmul(ps[:, 2 * p, c:c + 1], acc[c // 24][:, c % 24 * P:c % 24 * P + P], ones[:, 0:1],
                                start=True, stop=True)
            last.then_inc(full1[p], 1)
            for kh in range(2):
                project(5, kh)
            pe.wait_ge(s["lat_ready"], 1)
            p = free(pe, "latT")
            features(p, lambda k, h: latn[:, h, k * P:k * P + P], 3).then_inc(full1[p], 1)
            for name, ready, x in (("qTa", "q_ready", moba[0]), ("kTa", "k_ready", moba[1])):
                pe.wait_ge(s[ready], 1)
                p = free(pe, name)
                features(p, lambda k, h: x[:, h, k * P:k * P + P]).then_inc(full1[p], 1)
            moved(pe, "latT")
            pe.wait_ge(s["wuq_in"], 16)
            for h in range(HALVES):
                p = free(pe, f"qm{h}")
                for b, (c0, n) in enumerate(((0, 512), (512, 256))):
                    for k in range(2):
                        last = T.matmul(ps[:, 2 * p + b, 0:n], latT[:, k, h * P:h * P + P], wuq[:, k, c0:c0 + n],
                                        start=k == 0, stop=k == 1)
                last.then_inc(full1[p], 1)
            pe.wait_ge(s["wukv_in"], 16)
            for h in range(HALVES):
                p = free(pe, f"kv{h}")
                for b in range(2):
                    last = T.matmul(ps[:, 2 * p + b, :], latT[:, 2, h * P:h * P + P], wukv[:, b * 512:b * 512 + 512],
                                    start=True, stop=True)
                last.then_inc(full1[p], 1)

            def scores(h):
                bank = 2 * (h % 2)
                if h < HEADS:
                    q, k = [a[64 * (h % 2):64 * (h % 2) + HD, h // 2, :] for a in (qTa, kTa)]
                else:
                    q, k = qTb[0:QK, h - HEADS, :], kTb[0:QK, h - HEADS, :]
                if h >= 2:
                    pe.wait_ge(s["s_free"], h - 1)
                T.matmul(ps[:, bank, 0:P], q[:, 0:P], k[:, 0:P], start=True, stop=True)
                T.matmul(ps[:, bank, P:3 * P], q[:, P:S], k, start=True, stop=True).then_inc(s["s_full"], 1)

            def transpose_probs(h):
                bank = 2 * (h % 2) + 1
                pe.wait_ge(s["prob_done"], h + 1)
                if h >= 2:
                    pe.wait_ge(s["t_free"], h - 1)
                for b in range(3):
                    last = T.transpose(ps[:, bank, b * P:b * P + P], prob[:, h % 2, b * P:b * P + P], ident)
                last.then_inc(s["t_full"], 1)

            def weigh_values(h):
                c = h % HEADS * HD

                def v(half):
                    if h < HEADS:
                        return moba[2][:, half, c:c + HD]
                    return kv[:, half, (h - HEADS) * (NOPE + VD) + NOPE:(h - HEADS + 1) * (NOPE + VD)]
                pt = probT[:, h % 2, :]
                pe.wait_ge(s["t_free"], h + 1)
                T.matmul(ps[:, 6, c:c + HD], pt[:, 0:P], v(0), start=True, stop=True)
                T.matmul(ps[:, 7, c:c + HD], pt[:, P:2 * P], v(0), start=True, stop=False)
                T.matmul(ps[:, 7, c:c + HD], pt[:, 2 * P:3 * P], v(1), start=False, stop=True
                         ).then_inc(s["pv_done"], 1)

            for name in ("qTa", "kTa", "qm0", "qm1", "kv0", "v"):
                moved(pe, name)
            for h in range(HEADS + 2):
                if h < HEADS:
                    scores(h)
                    project(6 + h // 4, h // 2 % 2, (h % 2,))
                if 1 <= h <= HEADS:
                    transpose_probs(h - 1)
                if h >= 2:
                    weigh_values(h - 2)
            pe.wait_ge(s["t_free"], HEADS)
            pe.wait_ge(s["s_free"], HEADS)
            for tag, ready, x in (("qTb", "mlaq_ready", qm), ("kTb", "mlak_ready", km)):
                pe.wait_ge(s[ready], 1)
                for j in range(2):
                    p = free(pe, f"{tag}{j}")
                    features(p, lambda k, h: x[:, h, (4 * j + k) * QK:(4 * j + k + 1) * QK], w=QK
                             ).then_inc(full1[p], 1)
            for name in ("qTb0", "qTb1", "kTb0", "kTb1"):
                moved(pe, name)
            for h in range(HEADS, 2 * HEADS + 2):
                if h < 2 * HEADS:
                    scores(h)
                if HEADS + 1 <= h <= 2 * HEADS:
                    transpose_probs(h - 1)
                if h >= HEADS + 2:
                    if h == HEADS + 2:
                        pe.wait_ge(s["y_done"], 1)
                    weigh_values(h - 2)

            for br, name in enumerate(("yTa", "yTb")):
                pe.wait_ge(s["y_done"], br + 1)
                p = free(pe, name)
                if br:
                    pe.wait_ge(s["t_free"], 2 * HEADS)
                features(p, lambda k, h: HN[:, br, h * 512 + k * P:h * 512 + k * P + P]).then_inc(full1[p], 1)
            c = 2 * len(GROUP1)
            for g in range(2):
                for br, name in enumerate(("A", "B")):
                    chunk(c)
                    moved(pe, "yTb" if br else "yTa")
                    p = free(pe, f"{name}{g}")
                    for h in range(HALVES):
                        for k in range(4):
                            last = T.matmul(ps[:, 2 * p + h, :], HT[:, 4 * br + k, h * P:h * P + P],
                                            slot(c, 4, 512)[:, k, :], start=k == 0, stop=k == 3)
                    last.then_inc(s["chunk_used1"], 1)
                    c += 1
            for j in range(2):
                pe.wait_ge(s["merged_done"], j + 1)
                p = free(pe, f"mT{j}")
                features(p, lambda k, h: merged[:, h, (4 * j + k) * P:(4 * j + k + 1) * P]).then_inc(full1[p], 1)
            for g in range(2):
                for kh in range(2):
                    chunk(c)
                    moved(pe, f"mT{kh}")
                    p = free(pe, f"o{g}")
                    for h in range(HALVES):
                        for k in range(4):
                            last = T.matmul(ps[:, 2 * p + h, :], mT[:, 4 * kh + k, h * P:h * P + P],
                                            slot(c, 4, 512)[:, k, :], start=kh + k == 0, stop=4 * kh + k == KC - 1)
                    last.then_inc(s["chunk_used1"], 1)
                    c += 1
            pe.wait_ge(s["hn2_done"], 2)
            for j in range(2):
                p = free(pe, f"fT{j}")
                features(p, lambda k, h: HN[:, h, (4 * j + k) * P:(4 * j + k + 1) * P]).then_inc(full1[p], 1)
            moved(pe, "fT0")
            moved(pe, "fT1")
            pe.wait_ge(s["wr_in"], 16)
            p = free(pe, "rt")
            for h in range(HALVES):
                for k in range(KC):
                    last = T.matmul(ps[:, 2 * p, h * E:h * E + E], HT[:, k, h * P:h * P + P], wr[:, k, :],
                                    start=k == 0, stop=k == KC - 1)
            last.then_inc(full1[p], 1)
            pe.wait_ge(s["mask_done"], 2)
            p = free(pe, "pos")
            T.matmul(ps[:, 2 * p, 0:E], before, mask[:, 0, :], start=True, stop=True)
            T.matmul(ps[:, 2 * p, E:2 * E], ones, mask[:, 0, :], start=True, stop=False)
            T.matmul(ps[:, 2 * p, E:2 * E], before, mask[:, 1, :], start=False, stop=True)
            T.matmul(ps[:, 2 * p, 2 * E:3 * E], ones, mask[:, 0, :], start=True, stop=False)
            T.matmul(ps[:, 2 * p, 2 * E:3 * E], ones, mask[:, 1, :], start=False, stop=True).then_inc(full1[p], 1)

            def gather():
                for k in range(KC):
                    for h in range(HALVES):
                        last = T.matmul(ps[:, 2, k * CAP:k * CAP + CAP], HN[:, h, k * P:k * P + P], pick[:, h, :],
                                        start=h == 0, stop=h == HALVES - 1)
                last.then_inc(s["gather_done"], 1)

            def scatter(h):
                for g in range(2):
                    last = T.matmul(ps[:, 6 + g, :], scat[64 * g:64 * g + CAP, h, :], yslot[64 * g:64 * g + CAP, :],
                                    start=True, stop=True)
                last.then_inc(s["sc_ready"], 1)

            def side_by_side(bank, lhsT, w, start, stop):
                for g in range(2):
                    last = T.matmul(ps[64 * g:64 * g + CAP, bank, :], lhsT, w(g), start=start, stop=stop)
                return last

            pe.wait_ge(s["pick_ready"], 1)
            gather()
            pe.wait_ge(s["bias_in"], 32)
            extra = pe.value_load(nextra[0:1, 0:1], min_val=0, max_val=ROUNDS - 1)
            with pe.Fori(0, extra * E + E) as i:
                pe.wait_ge(s["xg_ready"], i + 1)
                pe.wait_ge(s["gu_used"], i + FIRST)
                for k in range(KC):
                    pe.wait_ge(ring2[k], i * 16 + 16)
                    side_by_side(0, xg[:, k, :], lambda g: ring[:, k, g * 512:g * 512 + 512], k == 0, False)
                    side_by_side(1, xg[:, k, :], lambda g: ring[:, k, F + g * 512:F + g * 512 + 512], k == 0, False
                                 ).then_inc(s["chunk_used2"], 1)
                    if k == 2:
                        pe.wait_ge(s["y_ready"], i + FIRST)
                        pe.wait_ge(s["scat_ready"], i + FIRST)
                        pe.wait_ge(s["sc_used"], i * 2 + FIRST)
                        scatter(0)
                    if k == 5:
                        pe.wait_ge(s["sc_used"], i * 2 + (1 + FIRST))
                        scatter(1)
                pe.wait_ge(s["esel_ready"], i + 1)
                side_by_side(0, esel[0:E, :], lambda g: bias[0:E, g * 512:g * 512 + 512], False, True)
                side_by_side(1, esel[0:E, :], lambda g: bias[0:E, F + g * 512:F + g * 512 + 512], False, True
                             ).then_inc(s["gu_ready"], 1)
                pe.wait_ge(s["pick_ready"], i + 2)
                gather()
                pe.wait_ge(s["pickw_ready"], i + 1)
                for h in range(HALVES):
                    last = T.transpose(ps[:, 4, h * P:h * P + P], pickw[:, h, :], ident)
                last.then_inc(s["scatT_done"], 1)
                pe.wait_ge(s["hid_ready"], i + 1)
                for c in range(4):
                    last = T.transpose(ps[:, 3, c * P:c * P + P], hid[:, c * P:c * P + P], ident)
                last.then_inc(s["hidT_full"], 1)
                pe.wait_ge(s["hidT_ready"], i + 1)
                pe.wait_ge(s["y_ready"], i + FIRST)
                for c in range(KC):
                    if c % 2 == 0:
                        pe.wait_ge(ring2[KC + c // 2], i * 16 + 16)
                    w = slot(KC + c // 2, 2, D)[:, c % 2, :]
                    at = c % 4 * P + c // 4 * CAP
                    last = side_by_side(5, hidT[:, at:at + CAP], lambda g: w[:, g * 512:g * 512 + 512], c == 0, False)
                    if c % 2:
                        last.then_inc(s["chunk_used2"], 1)
                side_by_side(5, esel[0:E, :], lambda g: bias[0:E, 2 * F + g * 512:2 * F + g * 512 + 512], False, True
                             ).then_inc(s["down_done"], 1)
            pe.wait_ge(s["y_ready"], extra * E + (E + FIRST))
            for h in range(HALVES):
                pe.wait_ge(s["sc_used"], extra * (2 * E) + (2 * E + h + FIRST))
                scatter(h)

            pe.wait_ge(s["p_in"], 16)
            p = U3["pT"][0]
            features(p, lambda k, h: pin[:, h, k * P:k * P + P], 2).then_inc(full3[p], 1)
            moved3_(pe, "pT")
            pe.wait_ge(ring3[0], 16)
            pe.wait_ge(s["hn3_done"], 2)
            for j in range(2):
                p = U3[f"hT{j}"][0]
                features(p, lambda k, h: HN[:, h, (4 * j + k) * P:(4 * j + k + 1) * P]).then_inc(full3[p], 1)
            for g in range(2):
                p = U3[f"pp{g}"][0]
                if g:
                    moved3_(pe, "hT0")
                for h in range(HALVES):
                    for k in range(2):
                        last = T.matmul(ps[:, 2 * p + h, :], pT[:, k, h * P:h * P + P],
                                        slot(0, 2, D)[:, k, g * 512:g * 512 + 512], start=k == 0, stop=k == 1)
            last.then_inc(s["chunk_used3"], 1)
            moved3_(pe, "hT1")
            for g in range(2):
                p = U3[f"g{g}"][0]
                for kh in range(2):
                    c = 1 + 2 * g + kh
                    pe.wait_ge(ring3[c], 16)
                    for h in range(HALVES):
                        for k in range(4):
                            last = T.matmul(ps[:, 2 * p + h, :], HT[:, 4 * kh + k, h * P:h * P + P],
                                            slot(c, 4, 512)[:, k, :], start=kh + k == 0, stop=4 * kh + k == KC - 1)
                    last.then_inc(s["chunk_used3"], 1)

            with pe.Fori(0, LAYERS) as l:
                def lfree(name):
                    p, _, moves, _ = UL[name]
                    pe.wait_ge(movedL[p], l * LM[p] + (moves + FIRST))
                    return p

                pe.wait_ge(s["l_hn"], l * 2 + 2)
                for j in range(2):
                    p = lfree(f"hT{j}")
                    features(p, lambda k, h: HN[:, h, (4 * j + k) * P:(4 * j + k + 1) * P]).then_inc(fullL[p], 1)
                movedL_(pe, l, "hT0")
                movedL_(pe, l, "hT1")

                def group(i):
                    p = lfree(GROUPL[i][0])
                    n = [PRE3 + 2 * i, PRE3 + 2 * i + 1]
                    for m in n:
                        pe.wait_ge(ring3[m % SLOTS], l * 16 + 16 * (m // SLOTS + 1))
                    for c in range(4):
                        for k in range(KC):
                            last = T.matmul(flat(p, S, c * S), slot(n[k // 4], 4, 512)[:, k % 4, c * P:c * P + P],
                                            HT[:, k, :], start=k == 0, stop=k == KC - 1)
                            if c == 3 and k % 4 == 3:
                                last.then_inc(s["chunk_used3"], 1)

                for i in range(3):
                    group(i)
                p = lfree("mix")
                pe.wait_ge(s["l_pooled"], l + 1)
                pe.wait_ge(s["wpool_in"], l * 16 + 16)
                for g in range(4):
                    last = T.matmul(flat(p, S, g * S), wpool[:, g, :], PL[:, g * S:g * S + S], start=True, stop=True)
                last.then_inc(fullL[p], 1)
                for i in range(3, 6):
                    group(i)
                p = lfree("gpb")
                pe.wait_ge(s["l_diag"], l + 1)
                for b in range(2):
                    last = T.matmul(ps[:, 2 * p + b, :], ones, diag[:, 2 * b:2 * b + 2, :], start=True, stop=True)
                last.then_inc(fullL[p], 1)
                pe.wait_ge(s["wo2_in"], l * 16 + 16)
                movedL_(pe, l, "mix")
                for part in range(2):
                    if part:
                        pe.wait_ge(s["l_conv"], l + 1)
                    for g in range(2):
                        p = UL[f"y{g}"][0]
                        if not part:
                            lfree(f"y{g}")
                        for h in range(HALVES):
                            for k in range(4):
                                c = 4 - 4 * part + k
                                last = T.matmul(ps[:, 2 * p + h, :], yT3[:, c, h * P:h * P + P],
                                                wo2[:, c, g * 512:g * 512 + 512], start=part + k == 0,
                                                stop=part == 1 and k == 3)
                        if part:
                            last.then_inc(fullL[p], 1)


_INS = ["x", "p", "g_mix", "w_in", "moba_q_norm", "moba_k_norm", "mla_q_lat_norm", "w_uq", "mla_kv_lat_norm", "w_ukv",
        "mla_q_norm", "mla_k_norm", "w_branch_a", "w_branch_b", "w_out", "g_ffn", "w_router", "b_router", "w_gate_up",
        "b_gate_up", "w_down", "b_down", "g_ple", "w_ple_gate", "w_ple_proj", "c_2", "w_ada_2", "b_ada_2", "g_pre_2",
        "w_in_2", "w_conv_2", "w_pool_2", "pool_scale_2", "w_out_2", "g_post_2"]


def kernel(**inputs):
    import numpy as _np
    import concourse.bacc as _bacc
    from concourse import mybir as _mybir
    from concourse.bass_utils import run_bass_kernel_spmd as _run

    nc = _bacc.Bacc("TRN2", target_bir_lowering=False, num_devices=1)
    arrays, t = {}, {}
    consts, inv = shape_constants()
    for name, a in [(n, inputs[n]) for n in _INS] + [("consts", consts), ("inv_windows", inv)]:
        a = _np.ascontiguousarray(a)
        arrays[f"in_{name}_dram"] = a
        t[name] = nc.dram_tensor(f"in_{name}_dram", a.shape, _mybir.dt.from_np(a.dtype), kind="ExternalInput").ap()
    out = nc.dram_tensor("out_dram", (1, S, D), _mybir.dt.float32, kind="ExternalOutput").ap()
    build(nc, t, out)
    r = _run(nc, [arrays], core_ids=[0])
    return r.results[0]["out_dram"]
```

```python
import numpy as np
import concourse.bass as bass
from concourse import mybir
from contextlib import ExitStack

P = 128
S, D = 256, 1024
HALVES = S // P
KC = D // P
HEADS, HD = 8, 64
QL, KVL, ROPE, QK = 256, 128, 32, 96
NOPE, VD = 64, 64
E, TOPK, F = 32, 4, 1024
CAP = 64
ROUNDS = S // CAP
PCOLS = ROUNDS * E
EPS = 1e-6
LIMIT, ALPHA = 7.0, 1.702
THETA = 10000.0
LAYERS = 2
ADA_EARLY = 3
NORMS = 8
NEG = -1e30
POOL_WINDOWS = (2, 4, 8, 16)
PAD = 16
SLOTS = 12
SLOT = 2048
SLOTS1 = 9
SLOTS3 = 8
HIGHS = 6

C_ID, C_BEFORE, C_ONES, C_SLOT = 0, P, 2 * P, 3 * P
C_CAUSAL = 4 * P
C_MCOS = C_CAUSAL + 3 * P
C_MSIN = C_MCOS + HALVES * HD
C_LCOS = C_MSIN + HALVES * HD
C_LSIN = C_LCOS + HALVES * ROPE
C_SEL = C_LSIN + HALVES * ROPE
C_THR = C_SEL + PCOLS
C_MHALF = C_THR + ROUNDS
NCONST = C_MHALF + 1

A_MIX, A_LAT, A_FFN, A_PLE = 0, 8, 11, 19
A_PRE, A_POST, A_CONV, A_PSC = 27, 43, 59, 83
NA = 91
B_ADA, B_C = 0, 48
NB = 56


def shape_constants():
    c = np.zeros((P, NCONST), np.float32)
    c[:, C_ID:C_ID + P] = np.eye(P)
    c[:, C_BEFORE:C_BEFORE + P] = np.triu(np.ones((P, P)), 1)
    c[:, C_ONES:C_ONES + P] = 1.0
    c[:, C_SLOT:C_SLOT + P] = np.tile(np.arange(CAP), 2)
    above = np.where(np.tril(np.ones((P, P))) > 0, 0.0, NEG)
    c[:, C_CAUSAL:C_CAUSAL + P] = above
    c[:, C_CAUSAL + 2 * P:C_CAUSAL + 3 * P] = above

    def rope(dim):
        half = dim // 2
        inv = np.float32(THETA) ** (-(np.arange(half, dtype=np.float32) / np.float32(half)))
        ang = np.arange(S, dtype=np.float32)[:, None] * inv[None, :].astype(np.float32)
        cos, sin = np.cos(ang), np.sin(ang)
        put = lambda a: a.reshape(HALVES, P, dim).transpose(1, 0, 2).reshape(P, HALVES * dim)
        return put(np.concatenate([cos, cos], 1)), put(np.concatenate([-sin, sin], 1))

    c[:, C_MCOS:C_MSIN], c[:, C_MSIN:C_LCOS] = rope(HD)
    c[:, C_LCOS:C_LSIN], c[:, C_LSIN:C_SEL] = rope(ROPE)
    for k in range(E):
        c[k, C_SEL + k:C_SEL + PCOLS:E] = 1.0
    c[:, C_THR:C_THR + ROUNDS] = (np.arange(ROUNDS) + 1) * CAP
    c[:, C_MHALF] = -0.5
    inv = np.stack([1.0 / np.minimum(np.arange(1, S + 1), w) for w in POOL_WINDOWS]).astype(np.float32)
    return c, np.ascontiguousarray(np.broadcast_to(inv.reshape(1, -1), (P, 4 * S)))


def build(nc, t, out):
    fp32, i32, u32 = mybir.dt.float32, mybir.dt.int32, mybir.dt.uint32
    ALU = mybir.AluOpType
    ACT = mybir.ActivationFunctionType
    AX = mybir.AxisListType.X
    V, G, A, T = nc.vector, nc.gpsimd, nc.scalar, nc.tensor
    ds = bass.ds

    ctx = ExitStack()
    with ctx:
        offsets = {}

        def sb(name, shape, dt=fp32):
            tile = ctx.enter_context(nc.sbuf_tensor(name, shape, dt))
            offsets[name] = nc.sbuf_base - 4 * int(np.prod(shape[1:]))
            return tile

        def rounded(name, of, shape, skip=0):
            return nc.alloc_sbuf_tensor_at(name, shape, mybir.dt.float32r, offset=offsets[of] + 4 * skip)

        def sem(name):
            return ctx.enter_context(nc.semaphore(name))

        ring = sb("ring", [P, SLOTS, SLOT])
        X = sb("X", [P, HALVES, D])
        HN = sb("HN", [P, HALVES, D])
        HT = sb("HT", [P, KC, S])
        const = sb("const", [P, NCONST])
        arena = sb("arena", [P, 72 * 256])
        w_low = rounded("w_low", "ring", [P, SLOTS3, SLOT])
        ring_highs = rounded("ring_highs", "ring", [P, SLOTS - SLOTS3, SLOT], SLOTS3 * SLOT)
        arena_highs = rounded("arena_highs", "arena", [P, 4, SLOT])
        HT_r, HN_r = rounded("HT_r", "HT", [P, KC, S]), rounded("HN_r", "HN", [P, KC, S])
        tabs = sb("tabs", [P, 4 * HALVES * HD + 4 * HALVES * ROPE])
        gains = sb("gains", [P, 2 * HD + 2 * QK + E])
        colA = sb("colA", [P, NA])
        colB = sb("colB", [P, NB])
        mods = sb("mods", [P, LAYERS, 24])
        wr = sb("wr", [P, KC, E])
        posm = sb("posm", [P, HALVES, PCOLS + 1])
        wtok = sb("wtok", [P, HALVES, PCOLS])
        st = sb("st", [P, 128])
        nextra = sb("nextra", [P, 1], i32)
        top_i = sb("top_i", [P, HALVES, 8], u32)
        ps = ctx.enter_context(nc.psum_tensor("ps", [P, 8, 512], fp32))

        def view(kb, n, pattern=None, **kw):
            a = arena[:, kb * 256:kb * 256 + n]
            return a.rearrange(pattern, **kw) if pattern else a

        ident = const[:, C_ID:C_ID + P]
        before = const[:, C_BEFORE:C_BEFORE + P]
        ones = const[:, C_ONES:C_ONES + P]
        slots = const[:, C_SLOT:C_SLOT + P]
        causal = const[:, C_CAUSAL:C_CAUSAL + 3 * P]

        hn_flat = HN[:].rearrange("p a b -> p (a b)")
        acc0, ada_ring = [ring[:, SLOTS1:SLOTS, :].rearrange("p a b -> p (a b)")[:, i * 3 * D:i * 3 * D + 3 * D]
                          .rearrange("p (h n) -> p h n", h=2) for i in range(2)]
        acc = [acc0, view(36, 3 * D, "p (h n) -> p h n", h=2)]
        gate = [view(0, HALVES * D, "p (a b) -> p a b", a=HALVES), view(24, HALVES * D, "p (a b) -> p a b", a=HALVES)]
        wukv = view(42, D)
        qTb = view(8, HEADS * S, "p (a b) -> p a b", a=HEADS)
        kTb = view(16, HEADS * S, "p (a b) -> p a b", a=HEADS)
        latT = [view(70, S), view(71, S), view(60, S)]
        mT = view(8, KC * S, "p (a b) -> p a b", a=KC)
        moba = [view(24 + 4 * i, HALVES * 512, "p (a b) -> p a b", a=HALVES) for i in range(3)]
        qTa = hn_flat[:, 0:D].rearrange("p (a b) -> p a b", a=4)
        kTa = hn_flat[:, D:2 * D].rearrange("p (a b) -> p a b", a=4)
        qm = view(36, HALVES * HEADS * QK, "p (a b) -> p a b", a=HALVES)
        km = view(42, HALVES * HEADS * QK, "p (a b) -> p a b", a=HALVES)
        wuq = view(48, 2 * 768, "p (a b) -> p a b", a=2)
        kv = view(48, HALVES * D, "p (a b) -> p a b", a=HALVES)
        merged = kv
        SQ = view(56, HALVES * 768)
        vec_rows = view(56, 2 * P, "p (a b) -> p a b", a=2)
        SW = view(62, 1024)
        lat = view(66, HALVES * 416, "p (a b) -> p a b", a=HALVES)
        prob = view(66, 2 * 384, "p (a b) -> p a b", a=2)
        probT = view(69, 2 * 384, "p (a b) -> p a b", a=2)
        lg, mask, ex, em, pm = [SQ[:, 64 * i:64 * i + 64].rearrange("p (a b) -> p a b", a=HALVES) for i in range(5)]
        top_v = SQ[:, 320:336].rearrange("p (a b) -> p a b", a=HALVES)
        top_f = SQ[:, 336:352].rearrange("p (a b) -> p a b", a=HALVES)

        xg = view(0, KC * CAP, "p (a b) -> p a b", a=KC)
        glu, sig, upc, hid, hidT = [view(2 + 2 * i, 512) for i in range(5)]
        bias = view(12, 3 * D)
        yslot = view(24, 512)
        scat = view(26, HALVES * P, "p (a b) -> p a b", a=HALVES)
        pick = view(27, HALVES * CAP, "p (a b) -> p a b", a=HALVES)
        pickw = view(28, HALVES * P, "p (a b) -> p a b", a=HALVES)
        esel = view(29, CAP)

        w_high = [ring_highs[:, i, :] for i in range(4)] + [arena_highs[:, i, :] for i in range(2)]
        xT_r, yT_r = [[arena_highs[:, i, :].rearrange("p (a b) -> p a b", a=KC), low[:]]
                      for i, low in ((2, HT_r), (3, HN_r))]
        W3 = PAD + S
        U = view(32, 4 * W3, "p (a b) -> p a b", a=4)
        WA = arena[:, 36 * 256 + 64:36 * 256 + 64 + 4 * W3].rearrange("p (a b) -> p a b", a=4)
        WB = arena[:, 40 * 256 + 128:40 * 256 + 128 + 4 * W3].rearrange("p (a b) -> p a b", a=4)
        diag, conv = WB[:, :, PAD:W3], WA[:, :, PAD:W3]
        PL, SG, T1, UA = [view(45 + 4 * i, D) for i in range(4)]
        Z = arena[:, 61 * 256:61 * 256 + 4 * (S + 2)].rearrange("p (a b) -> p a b", a=4)
        invw = arena[:, 65 * 256 + 32:65 * 256 + 32 + D]
        wpool = arena[:, 69 * 256 + 64:69 * 256 + 64 + 512].rearrange("p (a b) -> p a b", a=4)
        pin = view(57, HALVES * 256, "p (a b) -> p a b", a=HALVES)
        pT = view(59, 2 * S, "p (a b) -> p a b", a=2)
        yT3 = hn_flat.rearrange("p (a b) -> p a b", a=KC)

        TM = HALVES * HD
        mtab = [[tabs[:, (2 * i + j) * TM:(2 * i + j + 1) * TM] for j in range(2)] for i in range(2)]
        o = 4 * TM
        LT = HALVES * ROPE
        ltab = []
        for i in range(2):
            ltab.append([tabs[:, o + j * LT:o + (j + 1) * LT] for j in range(2)])
            o += 2 * LT
        g_mq, g_mk = gains[:, 0:HD], gains[:, HD:2 * HD]
        g_lq, g_lk = gains[:, 2 * HD:2 * HD + QK], gains[:, 2 * HD + QK:2 * HD + 2 * QK]
        b_rt = gains[:, 2 * HD + 2 * QK:2 * HD + 2 * QK + E]

        names = """x_in const_in vec_in gain_in wuq_in wukv_in wr_in bias_in p_in inv_in wpool_in
        out_stored dve_step pow_in pow_out tables_done
        x_sums hn_done c_sigmoid q_ready k_ready mlaq_ready mlak_ready
        s_full s_free scored prob_done t_full t_free pv_done y_done
        gates_open merged_done ffn_sums hn2_done lg_ready mask_done expd routed
        used_ada0 used_ada1 full_ada0 full_ada1 chunk_used1 chunk_used2 chunk_used3
        acc1_cleared pick_ready pickw_ready esel_ready xg_ready gather_done gu_ready gu_used
        g_ready mid_ready sig_ready hid_ready scatT_done scat_ready hidT_full hidT_ready
        down_done y_ready sc_ready sc_used
        pads_set ple_sums x_ready
        l_sums l_hn l_pooled l_gp_sig l_ga_sig l_conv l_diag l_ysum l_tmp l_step
        w_highs w_lows x_highs x_lows y_lows""".split()
        s = {n: sem(n) for n in names}
        ring1 = [sem(f"ring1_{i}") for i in range(SLOTS1)]
        ring2 = [sem(f"ring2_{i}") for i in range(SLOTS)]
        ring3 = [sem(f"ring3_{i}") for i in range(SLOTS3)]
        full1, moved1 = [sem(f"full1_{p}") for p in range(4)], [sem(f"moved1_{p}") for p in range(4)]
        full3, moved3 = [sem(f"full3_{p}") for p in range(4)], [sem(f"moved3_{p}") for p in range(4)]
        fullL, movedL = [sem(f"fullL_{p}") for p in range(4)], [sem(f"movedL_{p}") for p in range(4)]

        FIRST = 1

        def ordinals(uses):
            fills, moves, at = [0] * 4, [0] * 4, {}
            for name, p, chunks in uses:
                at[name] = (p, fills[p], moves[p], chunks)
                moves[p] += 1
                fills[p] += chunks is None
            return at, fills, moves
        N = None
        U1, _, _ = ordinals([("vec", 3, N), ("hT0", 0, N), ("hT1", 1, N), ("q", 2, 2), ("k", 3, 4), ("lat", 0, 6),
                             ("v", 1, 8), ("latT", 2, N), ("qm0", 3, N), ("qm1", 0, N), ("kv0", 1, N),
                             ("kv1", 2, N), ("ga0", 3, 10), ("ga1", 2, 12), ("qTa", 0, N), ("kTa", 1, N),
                             ("gb0", 2, 14), ("gb1", 2, 16), ("qTb0", 2, N), ("qTb1", 0, N),
                             ("kTb0", 1, N), ("kTb1", 2, N), ("ada0", 2, N), ("yTa", 2, N), ("yTb", 0, N),
                             ("A0", 1, 17), ("B0", 2, 18), ("A1", 3, 19), ("B1", 0, 20),
                             ("mT0", 1, N), ("mT1", 2, N), ("o0", 3, 22), ("o1", 0, 24),
                             ("fT0", 1, N), ("fT1", 2, N), ("rt", 3, N), ("pos", 0, N)])
        U3, _, _ = ordinals([("pT", 2, N), ("pp0", 0, 1), ("pp1", 2, 1), ("hT0", 1, N), ("hT1", 3, N),
                             ("g0", 1, 3), ("g1", 3, 5), ("ada1", 0, N)])
        UL, LF, LM = ordinals([("hT0", 0, N), ("hT1", 1, N), ("up", 2, 2), ("gp", 3, 4), ("ua", 0, 6), ("mix", 1, N),
                               ("ca", 2, 8), ("ba", 3, 10), ("ga", 0, 12), ("gpb", 1, N), ("y0", 2, 15), ("y1", 3, 16)])

        def filled(eng, name):
            p, fills, _, chunks = U1[name]
            if chunks:
                eng.wait_ge(s["chunk_used1"], chunks)
            else:
                eng.wait_ge(full1[p], fills + 1)
            return p

        def moved(eng, name):
            eng.wait_ge(moved1[U1[name][0]], U1[name][2] + 1)
            return U1[name][0]

        def free(pe, name):
            if U1[name][2]:
                pe.wait_ge(moved1[U1[name][0]], U1[name][2])
            return U1[name][0]

        def filled3(eng, name):
            p, fills, _, chunks = U3[name]
            if chunks:
                eng.wait_ge(s["chunk_used3"], chunks)
            else:
                eng.wait_ge(full3[p], fills + 1)
            return p

        def moved3_(eng, name):
            eng.wait_ge(moved3[U3[name][0]], U3[name][2] + 1)
            return U3[name][0]

        def filledL(eng, l, name):
            p, fills, _, chunks = UL[name]
            if chunks:
                eng.wait_ge(s["chunk_used3"], l * PER_LAYER + (PRE3 + chunks))
            else:
                eng.wait_ge(fullL[p], l * LF[p] + (fills + 1))
            return p

        def movedL_(eng, l, name):
            p, _, moves, _ = UL[name]
            eng.wait_ge(movedL[p], l * LM[p] + (moves + 1 + FIRST))
            return p

        def pair(p):
            return ps[:, 2 * p:2 * p + 2, :]

        def flat(p, n=1024, at=0):
            return ps[:, 2 * p:2 * p + 2, :].rearrange("p a b -> p (a b)")[:, at:at + n]

        def cols(a, i, l=None):
            return a[:, i:i + 1] if l is None else a[:, ds(l + i, 1)]

        mods_f = mods[:].rearrange("p a b -> p (a b)")

        def k_rows(w, r0, nk, c0, n):
            return w[0, r0:r0 + nk * P, c0:c0 + n].rearrange("(k p) n -> p k n", p=P)

        col_groups = [(0, 512), (512, 512), (1536, 416), (1024, 512),
                      (1952, 512), (2464, 512), (2976, 512), (3488, 512)]
        GROUP1 = ["q", "k", "lat", "v", "ga0", "ga1", "gb0", "gb1"]
        LSTEPS = 25
        chunks1 = []
        for c0, n in col_groups:
            for kh in range(2):
                chunks1.append((k_rows(t["w_in"], kh * 512, 4, c0, n), 4, n))
        for g in range(2):
            for w in (t["w_branch_a"], t["w_branch_b"]):
                chunks1.append((k_rows(w, 0, 4, g * 512, 512), 4, 512))
        for g in range(2):
            for kh in range(2):
                chunks1.append((k_rows(t["w_out"], kh * 512, 4, g * 512, 512), 4, 512))
        N1 = len(chunks1)

        chunks3 = [(k_rows(t["w_ple_proj"], 0, 2, 0, D), 2, D)]
        for g in range(2):
            for kh in range(2):
                chunks3.append((k_rows(t["w_ple_gate"], kh * 512, 4, g * 512, 512), 4, 512))
        PRE3 = len(chunks3)
        GROUPL = [("up", 4), ("gp", 5), ("ua", 0), ("ca", 2), ("ba", 1), ("ga", 3)]
        for l in range(LAYERS):
            for _, g in GROUPL:
                for kh in range(2):
                    chunks3.append((t["w_in_2"][l, kh * 512:kh * 512 + 512, g * 512:g * 512 + 512]
                                    .rearrange("(k p) n -> p k n", p=P), 4, 512))
            for c in (4, 0):
                for g in range(2):
                    chunks3.append((t["w_out_2"][l, c * P:c * P + 512, g * 512:g * 512 + 512]
                                    .rearrange("(k p) n -> p k n", p=P), 4, 512))
        PER_LAYER = (len(chunks3) - PRE3) // LAYERS
        assert PER_LAYER % SLOTS3 == 0 and PRE3 == 5

        def slot3(n, tile=ring):
            return tile[:, n % SLOTS3, :]

        def high_of(m):
            return w_high[(m - 4 if m >= 4 else m) % HIGHS]

        def chunk_parts(m):
            return [a.rearrange("p (a b) -> p a b", a=4) for a in (high_of(m), slot3(m + 1, w_low))]

        def slot1(n, a, b):
            return ring[:, n % SLOTS1, 0:a * b].rearrange("p (a b) -> p a b", a=a)

        def slot(i, a, b):
            return ring[:, i % SLOTS, 0:a * b].rearrange("p (a b) -> p a b", a=a)

        ada_v = t["w_ada_2"].rearrange("l (k p) n -> (l k) p n", p=P)
        gu_v = t["w_gate_up"].rearrange("a e (k p) n -> (a e) k p n", p=P)
        dn_v = t["w_down"].rearrange("a e (j k p) n -> (a e) j p k n", p=P, k=2)

        block = ctx.enter_context(nc.Block())

        @block.sync
        def _(sp):
            sp.dma_start(X[:], t["x"][0].rearrange("(h p) n -> p h n", p=P)).then_inc(s["x_in"], 16)
            sp.dma_start(const[:], t["consts"]).then_inc(s["const_in"], 16)
            sp.wait_ge(s["x_in"], 16)
            sp.wait_ge(s["vec_in"], 16 * 11)
            for n, (src, a, b) in enumerate(chunks1):
                if n >= SLOTS1:
                    sp.wait_ge(s["chunk_used1"], n - SLOTS1 + 1)
                sp.dma_start(slot1(n, a, b), src).then_inc(ring1[n % SLOTS1], 16)

            def expert(e, used):
                for j in range(SLOTS):
                    used(j)
                    if j < KC:
                        src = gu_v[ds(e, 1), j].rearrange("e p n -> (e p) n")
                        sp.dma_start(ring[:, j, :], src).then_inc(ring2[j], 16)
                    else:
                        src = dn_v[ds(e, 1), j - KC].rearrange("e p k n -> (e p) k n")
                        sp.dma_start(slot(j, 2, D), src).then_inc(ring2[j], 16)

            def phase1_left(j):
                if j < SLOTS1:
                    sp.wait_ge(s["chunk_used1"], max(n for n in range(N1) if n % SLOTS1 == j) + 1)
                else:
                    filled(sp, "ada0")
                    for hf in range(2):
                        sp.wait_ge(s[f"used_ada{hf}"], LAYERS * KC + FIRST)

            expert(0, phase1_left)
            with sp.Fori(0, E - 1) as before_e:
                expert(before_e + 1, lambda j: sp.wait_ge(s["chunk_used2"], before_e * SLOTS + (j + 1)))
            sp.wait_ge(s["routed"], 1)
            extra = sp.value_load(nextra[0:1, 0:1], min_val=0, max_val=ROUNDS - 1)
            with sp.If(extra > 0):
                with sp.Fori(0, extra) as r:
                    with sp.Fori(0, E) as e:
                        expert(e, lambda j: sp.wait_ge(s["chunk_used2"],
                                                       r * (E * SLOTS) + e * SLOTS + ((E - 1) * SLOTS + j + 1)))
            for n, (src, a, b) in enumerate(chunks3):
                if n < SLOTS3:
                    sp.wait_ge(s["chunk_used2"], extra * (E * SLOTS) + ((E - 1) * SLOTS + n + 1))
                else:
                    sp.wait_ge(s["chunk_used3"], n - SLOTS3 + 1)
                sp.dma_start(slot3(n).rearrange("p (a b) -> p a b", a=a), src).then_inc(ring3[n % SLOTS3], 16)
            sp.wait_ge(s["x_ready"], 1 + LAYERS)
            sp.dma_start(out[0].rearrange("(h p) n -> p h n", p=P), X[:]).then_inc(s["out_stored"], 16)
            sp.wait_ge(s["out_stored"], 16)

        @block.gpsimd
        def _(pool):
            for hf in range(2):
                G.memset(acc[0][:, hf, :], 0.0).then_inc(s[f"used_ada{hf}"], FIRST)
            for a in [s[n] for n in ("down_done", "scatT_done", "gu_used", "sc_used")] + movedL:
                pool.sem_inc(a, FIRST)
            pool.wait_ge(s["const_in"], 16)
            pool.wait_ge(s["gain_in"], 16 * 5)

            def b2(a, w):
                return a.unsqueeze(1).to_broadcast([P, HALVES, w])

            def hv(a):
                return a.rearrange("p (h w) -> p h w", h=HALVES)

            def table(dst, cos, sin, g, w):
                G.tensor_tensor(hv(dst[0]), hv(cos), b2(g, w), ALU.mult)
                h = w // 2
                G.tensor_tensor(hv(dst[1])[:, :, 0:h], hv(sin)[:, :, 0:h], b2(g[:, h:w], h), ALU.mult)
                return G.tensor_tensor(hv(dst[1])[:, :, h:w], hv(sin)[:, :, h:w], b2(g[:, 0:h], h), ALU.mult)
            for i, g in ((0, g_mq), (1, g_mk)):
                table(mtab[i], const[:, C_MCOS:C_MSIN], const[:, C_MSIN:C_LCOS], g, HD)
            for i, g in ((0, g_lq), (1, g_lk)):
                last = table(ltab[i], const[:, C_LCOS:C_LSIN], const[:, C_LSIN:C_SEL], g[:, NOPE:QK], ROPE)
            last.then_inc(s["tables_done"], 1)

            powers = [0]

            def power(w0, n):
                powers[0] += 1
                pool.wait_ge(s["pow_in"], powers[0])
                G.tensor_tensor(st[:, w0:w0 + n], st[:, w0:w0 + n],
                                const[:, C_MHALF:C_MHALF + 1].to_broadcast([P, n]),
                                ALU.pow).then_inc(s["pow_out"], 1)

            def ada(layer, k0, k1):
                with pool.Fori(layer * KC + k0, layer * KC + k1) as i:
                    for hf in range(2):
                        pool.wait_ge(s[f"used_ada{hf}"], i + FIRST)
                        pool.dma_start(ada_ring[:, hf, :],
                                       ada_v[ds(i, 1), :, hf * 1536:hf * 1536 + 1536].rearrange("l p n -> (l p) n")
                                       ).then_inc(s[f"full_ada{hf}"], 16)

            power(0, 2)
            ada(0, 0, ADA_EARLY + 1)
            power(0, 4)
            power(16, 16)
            power(32, 16)
            power(16, 16)
            power(32, 16)
            ada(0, ADA_EARLY + 1, KC)
            ada(1, 0, 1)
            pool.wait_ge(s["y_done"], 2)
            for hf in range(2):
                G.memset(acc[1][:, hf, :], 0.0).then_inc(s["acc1_cleared"], 1)
            ada(1, 1, KC)
            pool.wait_ge(s["chunk_used1"], N1)
            pool.dma_start(bias[0:E, 0:2 * F], t["b_gate_up"][0]).then_inc(s["bias_in"], 16)
            pool.dma_start(bias[0:E, 2 * F:2 * F + D], t["b_down"][0]).then_inc(s["bias_in"], 16)
            power(0, 2)
            pool.wait_ge(s["routed"], 1)
            pool.dma_start(pin, t["p"][0, 0].rearrange("(h p) n -> p h n", p=P)).then_inc(s["p_in"], 16)
            pool.dma_start(invw, t["inv_windows"]).then_inc(s["inv_in"], 16)
            for z, n in ((U, PAD), (Z, 2)):
                G.memset(z[:, :, 0:n], 0.0).then_inc(s["pads_set"], 1)
            power(0, 2)
            filled3(pool, "ada1")
            for z in (WA, WB):
                G.memset(z[:, :, 0:PAD], 0.0).then_inc(s["pads_set"], 1)
            with pool.Fori(0, LAYERS) as l:
                pool.wait_ge(movedL[1], l * LM[1] + FIRST)
                pool.dma_start(wpool, t["w_pool_2"][ds(l, 1)].rearrange("l g c d -> c (l g) d")
                               ).then_inc(s["wpool_in"], 16)
                for i in range(2):
                    pool.wait_ge(s["pow_in"], l * 2 + (powers[0] + i + 1))
                    G.tensor_tensor(st[:, 0:2], st[:, 0:2], const[:, C_MHALF:C_MHALF + 1].to_broadcast([P, 2]),
                                    ALU.pow).then_inc(s["pow_out"], 1)

        @block.scalar
        def _(act):
            rows = [(t["g_mix"].rearrange("a (k n) -> (a k) n", n=P), 0, A_MIX),
                    (t["mla_q_lat_norm"].rearrange("a (k n) -> (a k) n", n=P), 0, A_LAT),
                    (t["mla_kv_lat_norm"].rearrange("a (k n) -> (a k) n", n=P), 0, A_LAT + 2),
                    (t["g_ffn"].rearrange("a (k n) -> (a k) n", n=P), 0, A_FFN),
                    (t["g_ple"].rearrange("a (k n) -> (a k) n", n=P), 0, A_PLE),
                    (t["g_pre_2"].rearrange("a (k n) -> (a k) n", n=P), 0, A_PRE),
                    (t["g_post_2"].rearrange("a (k n) -> (a k) n", n=P), 0, A_POST),
                    (t["w_conv_2"].rearrange("l k (c n) -> (l k c) n", n=P), 0, A_CONV),
                    (t["pool_scale_2"].rearrange("l (c n) -> (l c) n", n=P), 0, A_PSC),
                    (t["b_ada_2"].rearrange("l (c n) -> (l c) n", n=P), 1, B_ADA),
                    (t["c_2"].rearrange("a (k n) -> (a k) n", n=P), 1, B_C)]
            for src, i, r in rows:
                act.dma_start(vec_rows[r:r + src.shape[0], i, :], src).then_inc(s["vec_in"], 16)
            for dst, src in ((g_mq, t["moba_q_norm"]), (g_mk, t["moba_k_norm"]), (g_lq, t["mla_q_norm"]),
                             (g_lk, t["mla_k_norm"]), (b_rt, t["b_router"])):
                act.dma_start(dst, src[0].partition_broadcast(P)).then_inc(s["gain_in"], 16)
            act.dma_start(wuq, t["w_uq"][0].rearrange("(k p) n -> p k n", p=P)).then_inc(s["wuq_in"], 16)
            act.dma_start(wukv, t["w_ukv"][0]).then_inc(s["wukv_in"], 16)
            act.dma_start(wr[:], t["w_router"][0].rearrange("(k p) n -> p k n", p=P)).then_inc(s["wr_in"], 16)

            act.wait_ge(s["x_in"], 16)
            for h in range(HALVES):
                A.activation(HN[:, h, :], X[:, h, :], ACT.Square, accum_out=st[:, h:h + 1]).then_inc(s["x_sums"], 1)
            p = filled(act, "vec")
            A.copy(colA[:], ps[:, 2 * p, 0:NA])
            A.copy(colB[:], ps[:, 2 * p + 1, 0:NB]).then_inc(moved1[p], 1)
            act.wait_ge(moved1[p], 1)
            A.activation(st[:, 100:108], colB[:, B_C:B_C + KC], ACT.Sigmoid).then_inc(s["c_sigmoid"], 1)

            def scaled(p, done, dst, n, gain):
                for i in range(n):
                    last = A.activation(dst(i), flat(p, S, i * S), ACT.Copy, scale=gain(i))
                last.then_inc(done[p], 1)

            for j in range(2):
                scaled(filled(act, f"hT{j}"), moved1, lambda i: HT[:, 4 * j + i, :], 4,
                       lambda i: cols(colA, A_MIX + 4 * j + i))

            def move(name, dst, src):
                p = filled(act, name)
                A.copy(dst, src(p)).then_inc(moved1[p], 1)

            move("q", moba[0], pair)
            move("k", moba[1], pair)
            move("lat", lat, lambda p: pair(p)[:, :, 0:416])
            move("v", moba[2], pair)
            scaled(filled(act, "latT"), moved1, lambda i: latT[i], 3, lambda i: cols(colA, A_LAT + i))
            act.wait_ge(s["pow_out"], 2)
            for h in range(HALVES):
                p = filled(act, f"qm{h}")
                A.activation(qm[:, h, :], flat(p, 768), ACT.Copy, scale=st[:, h:h + 1]).then_inc(moved1[p], 1)
            for h in range(HALVES):
                p = filled(act, f"kv{h}")
                A.activation(kv[:, h, :], flat(p), ACT.Copy, scale=st[:, 2 + h:3 + h]).then_inc(moved1[p], 1)
            for name, dst in (("qTa", qTa), ("kTa", kTa)):
                move(name, dst, lambda p: flat(p).rearrange("p (a b) -> p a b", a=4))
            for g in range(2):
                move(f"ga{g}", gate[0][:, :, g * 512:g * 512 + 512], pair)
            for h in range(2 * HEADS):
                b, scale = h % 2, (HD if h < HEADS else QK) ** -0.5
                act.wait_ge(s["scored"], h + 1)
                c = 64 + h // HEADS * 16 + h % HEADS
                A.activation(prob[:, b, 0:P], prob[:, b, 0:P], ACT.Exp, bias=st[:, 48 + 2 * b:49 + 2 * b],
                             scale=scale, accum_out=st[:, c:c + 1])
                A.activation(prob[:, b, P:3 * P], prob[:, b, P:3 * P], ACT.Exp, bias=st[:, 49 + 2 * b:50 + 2 * b],
                             scale=scale, accum_out=st[:, c + 8:c + 9]).then_inc(s["prob_done"], 1)
                if h in (3, 7):
                    move(f"gb{h // 4}", gate[1][:, :, h // 4 * 512:h // 4 * 512 + 512], pair)
                if h == HEADS - 1:
                    for dst, tag in ((qTb, "qTb"), (kTb, "kTb")):
                        for j in range(2):
                            move(f"{tag}{j}", dst[0:QK, 4 * j:4 * j + 4, :],
                                 lambda p: flat(p)[0:QK].rearrange("p (a b) -> p a b", a=4))
            move("yTa", HT[:, 0:4, :].rearrange("p a b -> p (a b)"), flat)
            move("yTb", HT[:, 4:8, :].rearrange("p a b -> p (a b)"), flat)
            for i in range(2):
                A.activation(gate[i], gate[i], ACT.Sigmoid).then_inc(s["gates_open"], 1)
            for j in range(2):
                move(f"mT{j}", mT[:, 4 * j:4 * j + 4, :].rearrange("p a b -> p (a b)"), flat)
            moved(act, "o0")
            moved(act, "o1")
            scaled(filled(act, "fT0"), moved1, lambda i: HT[:, i, :], 4, lambda i: cols(colA, A_FFN + i))
            for h in range(HALVES):
                A.activation(HN[:, h, :], X[:, h, :], ACT.Square, accum_out=st[:, h:h + 1]).then_inc(s["ffn_sums"], 1)
            act.wait_ge(s["lg_ready"], 1)
            for h in range(HALVES):
                A.activation(ex[:, h, :], lg[:, h, :], ACT.Exp, bias=st[:, 4 + h:5 + h]).then_inc(s["expd"], 1)

            act.wait_ge(s["routed"], 1)
            extra = act.value_load(nextra[0:1, 0:1], min_val=0, max_val=ROUNDS - 1)
            with act.Fori(0, extra * E + E) as i:
                act.wait_ge(s["g_ready"], i + 1)
                A.activation(sig, glu, ACT.Sigmoid, scale=ALPHA).then_inc(s["sig_ready"], 1)
                act.wait_ge(s["hidT_full"], i + 1)
                A.copy(hidT, ps[:, 3, :]).then_inc(s["hidT_ready"], 1)
                act.wait_ge(s["scatT_done"], i + (1 + FIRST))
                act.wait_ge(s["sc_ready"], i * 2 + 2)
                A.copy(scat, ps[:, 4, 0:HALVES * P].rearrange("p (a b) -> p a b", a=HALVES)
                       ).then_inc(s["scat_ready"], 1)
                act.wait_ge(s["down_done"], i + (1 + FIRST))
                A.copy(yslot, ps[:, 5, :]).then_inc(s["y_ready"], 1)

            p = filled3(act, "pT")
            A.copy(pT, flat(p, 512).rearrange("p (a b) -> p a b", a=2)).then_inc(moved3[p], 1)
            act.wait_ge(s["chunk_used2"], extra * (E * SLOTS) + E * SLOTS)

            def w_split(m, l=None):
                n = m + 1
                if l is None:
                    act.wait_ge(ring3[n % SLOTS3], 16)
                else:
                    act.wait_ge(ring3[n % SLOTS3], l * (16 * PER_LAYER // SLOTS3) + 16 * (n // SLOTS3 + 1))
                    act.wait_ge(s["chunk_used3"], l * PER_LAYER + (m - 4 if m - 4 >= HIGHS else min(m - 4, 3) + 2))
                A.copy(high_of(m), slot3(n)).then_inc(s["w_highs"], 1)

            def x_split(j):
                A.copy(xT_r[0][:, 4 * j:4 * j + 4, :], HT[:, 4 * j:4 * j + 4, :]).then_inc(s["x_highs"], 1)

            for j in range(2):
                scaled(filled3(act, f"hT{j}"), moved3, lambda i: HT[:, 4 * j + i, :], 4,
                       lambda i: cols(colA, A_PLE + 4 * j + i))
                moved3_(act, f"hT{j}")
                x_split(j)
            w_split(0)
            w_split(1)
            for h in range(HALVES):
                A.activation(HN[:, h, :], X[:, h, :], ACT.Square, accum_out=st[:, h:h + 1]).then_inc(s["ple_sums"], 1)
            w_split(2)
            w_split(3)
            act.wait_ge(s["pow_out"], NORMS)
            for g in range(2):
                p = filled3(act, f"g{g}")
                if g:
                    act.wait_ge(s["l_tmp"], 1)
                for h in range(HALVES):
                    last = A.activation(SG[:, h * 512:h * 512 + 512], ps[:, 2 * p + h, :], ACT.Sigmoid,
                                        scale=st[:, h:h + 1])
                last.then_inc(moved3[p], 1)

            with act.Fori(0, LAYERS) as l:
                w_split(4, l)
                w_split(5, l)
                act.wait_ge(s["x_ready"], l + 1)
                for h in range(HALVES):
                    A.activation(HN[:, h, :], X[:, h, :], ACT.Square,
                                 accum_out=st[:, h:h + 1]).then_inc(s["l_sums"], 1)
                p = filledL(act, l, "hT0")
                for k in range(4):
                    last = A.activation(HT[:, k, :], flat(p, S, k * S), ACT.Identity,
                                        bias=cols(mods_f, k, l * 24), scale=cols(mods_f, 8 + k, l * 24))
                last.then_inc(movedL[p], 1)
                movedL_(act, l, "hT0")
                x_split(0)
                for m in (6, 7, 8, 9):
                    w_split(m, l)
                p = filledL(act, l, "up")
                act.wait_ge(s["pads_set"], 4)
                A.copy(U[:, :, PAD:W3], flat(p).rearrange("p (a b) -> p a b", a=4)).then_inc(movedL[p], 1)
                w_split(10, l)
                w_split(11, l)
                p = filledL(act, l, "gp")
                A.activation(SG, flat(p), ACT.Sigmoid).then_inc(s["l_gp_sig"], 1)
                w_split(12, l)
                w_split(13, l)
                p = filledL(act, l, "ua")
                A.copy(UA, flat(p)).then_inc(movedL[p], 1)
                for m in (14, 15, 16, 17, 18, 19):
                    w_split(m, l)
                p = filledL(act, l, "ga")
                movedL_(act, l, "gp")
                A.activation(SG, flat(p), ACT.Sigmoid).then_inc(s["l_ga_sig"], 1)
                p = filledL(act, l, "gpb")
                movedL_(act, l, "ca")
                A.copy(UA, flat(p)).then_inc(movedL[p], 1)
                act.wait_ge(s["l_conv"], l + 1)
                for g in range(2):
                    p = filledL(act, l, f"y{g}")
                    for h in range(HALVES):
                        if g:
                            act.wait_ge(s["l_ysum"], l * 4 + (h + 1))
                        A.activation(SG[:, h * 512:h * 512 + 512], ps[:, 2 * p + h, :], ACT.Square,
                                     accum_out=st[:, 8 + 2 * h + g:9 + 2 * h + g]).then_inc(s["l_ysum"], 1)

        @block.vector
        def _(dve):
            steps = [0]

            def run(ins):
                steps[0] += 1
                ins.then_inc(s["dve_step"], 1)

            def join():
                dve.wait_ge(s["dve_step"], steps[0])

            powers = [0]

            def power():
                powers[0] += 1
                dve.wait_ge(s["pow_out"], powers[0])

            dve.wait_ge(s["x_sums"], 2)
            V.tensor_scalar(st[:, 0:2], st[:, 0:2], 1.0 / D, EPS, ALU.mult, ALU.add).then_inc(s["pow_in"], 1)
            power()
            for h in range(HALVES):
                V.tensor_scalar(HN[:, h, :], X[:, h, :], st[:, h:h + 1], None, ALU.mult).then_inc(s["hn_done"], 1)
            dve.wait_ge(s["c_sigmoid"], 1)
            cact = st[:, 108:116]
            run(V.tensor_tensor(cact, st[:, 100:108], colB[:, B_C:B_C + KC], ALU.mult))
            join()

            def ada_half(layer, k, hf):
                a, n = acc[layer][:, hf, :], layer * KC + k
                dve.wait_ge(s[f"full_ada{hf}"], n * 16 + 16)
                dve.wait_ge(s[f"used_ada{hf}"], n + FIRST)
                V.scalar_tensor_tensor(a, ada_ring[:, hf, :], cact[:, k:k + 1], a, ALU.mult,
                                       ALU.add).then_inc(s[f"used_ada{hf}"], 1)

            def ada(layer, k0, k1):
                for k in range(k0, k1):
                    for hf in range(2):
                        ada_half(layer, k, hf)

            def mod_columns(l, p, done, n):
                m = mods[:, l, :]
                V.tensor_tensor(m, ps[:, 2 * p, 0:24], colB[:, B_ADA + 24 * l:B_ADA + 24 * l + 24],
                                ALU.add).then_inc(done[p], 1)
                dve.wait_ge(done[p], n)
                run(V.scalar_tensor_tensor(m[:, 8:16], m[:, 8:16], 1.0, colA[:, A_PRE + 8 * l:A_PRE + 8 * l + 8],
                                           ALU.add, ALU.mult))
                run(V.tensor_tensor(m[:, 16:24], m[:, 16:24], colA[:, A_POST + 8 * l:A_POST + 8 * l + 8], ALU.mult))
                join()

            def mean_squares(x, w, n0):
                xs = x.rearrange("p a (h d) -> p (a h) d", d=w)
                sq = SQ[:, 0:HALVES * HEADS * w].rearrange("p (a d) -> p a d", d=w)
                run(V.tensor_tensor(sq, xs, xs, ALU.mult))
                join()
                run(V.tensor_reduce(st[:, n0:n0 + 16], sq, AX, ALU.add))
                join()
                V.tensor_scalar(st[:, n0:n0 + 16], st[:, n0:n0 + 16], 1.0 / w, EPS, ALU.mult,
                                ALU.add).then_inc(s["pow_in"], 1)

            def unit_heads(x, w, n0):
                power()
                xs = x.rearrange("p a (h d) -> p (a h) d", d=w)
                run(V.tensor_tensor(xs, xs, st[:, n0:n0 + 16].unsqueeze(2).to_broadcast([P, 16, w]), ALU.mult))
                join()

            def rope(x, tab, w, done):
                h = w // 2
                sw = SW[:, 0:HALVES * HEADS * w].rearrange("p (a h d) -> p a h d", a=HALVES, h=HEADS)
                tb = [a.rearrange("p (a d) -> p a d", a=HALVES).unsqueeze(2) for a in tab]
                run(V.tensor_tensor(sw[:, :, :, 0:h], x[:, :, :, h:w],
                                    tb[1][:, :, :, 0:h].to_broadcast([P, HALVES, HEADS, h]), ALU.mult))
                run(V.tensor_tensor(sw[:, :, :, h:w], x[:, :, :, 0:h],
                                    tb[1][:, :, :, h:w].to_broadcast([P, HALVES, HEADS, h]), ALU.mult))
                join()
                run(V.tensor_tensor(x, x, tb[0].to_broadcast([P, HALVES, HEADS, w]), ALU.mult))
                join()
                V.tensor_tensor(x, x, sw, ALU.add).then_inc(s[done], 1)
                dve.wait_ge(s[done], 1)

            def four(x, d):
                return x.rearrange("p a (h d) -> p a h d", d=d)

            ada(0, 0, ADA_EARLY)
            dve.wait_ge(s["tables_done"], 1)

            def moba_ready(i, raw, done):
                moved(dve, raw)
                mean_squares(moba[i], HD, 16 + 16 * i)
                unit_heads(moba[i], HD, 16 + 16 * i)
                rope(four(moba[i], HD), mtab[i], HD, done)

            moved(dve, "lat")
            sq = SQ[:, 0:HALVES * 384].rearrange("p (a b) -> p a b", a=HALVES)
            run(V.tensor_tensor(sq, lat[:, :, 0:384], lat[:, :, 0:384], ALU.mult))
            join()
            run(V.tensor_reduce(st[:, 0:2], sq[:, :, 0:QL], AX, ALU.add))
            run(V.tensor_reduce(st[:, 2:4], sq[:, :, QL:384], AX, ALU.add))
            join()
            run(V.tensor_scalar(st[:, 0:2], st[:, 0:2], 1.0 / QL, EPS, ALU.mult, ALU.add))
            V.tensor_scalar(st[:, 2:4], st[:, 2:4], 1.0 / KVL, EPS, ALU.mult, ALU.add).then_inc(s["pow_in"], 1)
            power()
            moba_ready(0, "q", "q_ready")
            moba_ready(1, "k", "k_ready")
            moved(dve, "kv0")
            moved(dve, "kv1")
            kvh = kv.rearrange("p a (h d) -> p (a h) d", d=NOPE + VD)
            run(V.tensor_copy(km.rearrange("p a (h d) -> p (a h) d", d=QK)[:, :, 0:NOPE], kvh[:, :, 0:NOPE]))
            run(V.tensor_copy(four(km, QK)[:, :, :, NOPE:QK],
                              lat[:, :, 384:416].unsqueeze(2).to_broadcast([P, HALVES, HEADS, ROPE])))
            join()

            def mla_step(i):
                x, tag, g = ((qm, "mlaq_ready", g_lq), (km, "mlak_ready", g_lk))[i // 3]
                if i == 0:
                    moved(dve, "qm0")
                    moved(dve, "qm1")
                if i % 3 == 0:
                    mean_squares(x, QK, 16 + 16 * (i // 3))
                elif i % 3 == 1:
                    unit_heads(x, QK, 16 + 16 * (i // 3))
                else:
                    xs = x.rearrange("p a (h d) -> p (a h) d", d=QK)
                    run(V.tensor_tensor(xs[:, :, 0:NOPE], xs[:, :, 0:NOPE],
                                        g[:, 0:NOPE].unsqueeze(1).to_broadcast([P, 16, NOPE]), ALU.mult))
                    rope(four(x, QK)[:, :, :, NOPE:QK], ltab[i // 3], ROPE, tag)

            def score(h):
                b, scale = h % 2, (HD if h < HEADS else QK) ** -0.5
                bank = 2 * b
                dve.wait_ge(s["s_full"], h + 1)
                if h >= 2:
                    dve.wait_ge(s["t_full"], h - 1)
                run(V.tensor_tensor_reduce(out=prob[:, b, 0:P], in0=ps[:, bank, 0:P], in1=causal[:, 0:P], scale=1.0,
                                           scalar=-3e38, op0=ALU.add, op1=ALU.max,
                                           accum_out=st[:, 48 + 2 * b:49 + 2 * b]))
                V.tensor_tensor_reduce(out=prob[:, b, P:3 * P], in0=ps[:, bank, P:3 * P], in1=causal[:, P:3 * P],
                                       scale=1.0, scalar=-3e38, op0=ALU.add, op1=ALU.max,
                                       accum_out=st[:, 49 + 2 * b:50 + 2 * b]).then_inc(s["s_free"], 1)
                dve.wait_ge(s["s_free"], h + 1)
                join()
                V.tensor_scalar(st[:, 48 + 2 * b:50 + 2 * b], st[:, 48 + 2 * b:50 + 2 * b], -scale, None,
                                ALU.mult).then_inc(s["scored"], 1)

            def out_of_t(h):
                dve.wait_ge(s["t_full"], h + 1)
                if h >= 2:
                    dve.wait_ge(s["pv_done"], h - 1)
                V.tensor_copy(probT[:, h % 2, :], ps[:, 2 * (h % 2) + 1, 0:3 * P]).then_inc(s["t_free"], 1)

            def normalise(br):
                dve.wait_ge(s["pv_done"], HEADS * (br + 1))
                r = st[:, 64 + 16 * br:80 + 16 * br]
                run(V.reciprocal(r, r))
                join()
                V.tensor_tensor(HN[:, br, :].rearrange("p (a d) -> p a d", d=HD),
                                flat(3).rearrange("p (a d) -> p a d", d=HD),
                                r.unsqueeze(2).to_broadcast([P, 16, HD]), ALU.mult).then_inc(s["y_done"], 1)

            late_ada = [(k, hf) for k in range(ADA_EARLY, KC) for hf in range(2)]
            for h0 in (0, HEADS):
                for h in range(h0, h0 + HEADS + 1):
                    if h < h0 + HEADS:
                        score(h)
                    if h > h0:
                        out_of_t(h - 1)
                    if h0 == 0 and h < 6:
                        mla_step(h)
                    if late_ada and h >= 6:
                        ada_half(0, *late_ada.pop(0))
                if h0:
                    mod_columns(0, filled(dve, "ada0"), moved1, U1["ada0"][2] + 1)
                normalise(h0 // HEADS)

            dve.wait_ge(s["gates_open"], 2)
            dve.wait_ge(s["acc1_cleared"], 2)
            tmp = SQ[:, 0:HALVES * 512].rearrange("p (a b) -> p a b", a=HALVES)
            for g in range(2):
                part = slice(g * 512, g * 512 + 512)
                ada(1, 2 * g, 2 * g + 2)
                p = filled(dve, f"A{g}")
                V.tensor_tensor(merged[:, :, part], gate[0][:, :, part], pair(p), ALU.mult).then_inc(moved1[p], 1)
                moved(dve, f"A{g}")
                p = filled(dve, f"B{g}")
                V.tensor_tensor(tmp, gate[1][:, :, part], pair(p), ALU.mult).then_inc(moved1[p], 1)
                moved(dve, f"B{g}")
                V.tensor_tensor(merged[:, :, part], merged[:, :, part], tmp, ALU.add).then_inc(s["merged_done"], 1)
                dve.wait_ge(s["merged_done"], g + 1)
            ada(1, 4, KC)
            for g in range(2):
                p = filled(dve, f"o{g}")
                part = X[:, :, g * 512:g * 512 + 512]
                V.tensor_tensor(part, part, pair(p), ALU.add).then_inc(moved1[p], 1)
            p = filled(dve, "fT1")
            for i in range(4):
                last = V.tensor_scalar(HT[:, 4 + i, :], flat(p, S, i * S), cols(colA, A_FFN + 4 + i), None, ALU.mult)
            last.then_inc(moved1[p], 1)
            dve.wait_ge(s["ffn_sums"], 2)
            V.tensor_scalar(st[:, 0:2], st[:, 0:2], 1.0 / D, EPS, ALU.mult, ALU.add).then_inc(s["pow_in"], 1)
            power()
            for h in range(HALVES):
                V.tensor_scalar(HN[:, h, :], X[:, h, :], st[:, h:h + 1], None, ALU.mult).then_inc(s["hn2_done"], 1)

            p = filled(dve, "rt")
            for h in range(HALVES):
                last = V.scalar_tensor_tensor(lg[:, h, :], ps[:, 2 * p, h * E:h * E + E], st[:, h:h + 1], b_rt,
                                              ALU.mult, ALU.add)
            last.then_inc(moved1[p], 1)
            moved(dve, "rt")
            for h in range(HALVES):
                run(V.max(top_v[:, h, :], lg[:, h, :]))
            join()
            for h in range(HALVES):
                run(V.max_index(top_i[:, h, :], top_v[:, h, :], lg[:, h, :]))
            V.tensor_scalar(st[:, 4:6], top_v[:, :, 0], -1.0, None, ALU.mult).then_inc(s["lg_ready"], 1)
            join()
            run(V.tensor_copy(top_f, top_i[:]))
            join()
            for j in range(TOPK):
                for h in range(HALVES):
                    idx = top_f[:, h, j:j + 1]
                    if j == 0:
                        ins = V.tensor_scalar(mask[:, h, :], slots[:, 0:E], idx, None, ALU.is_equal)
                    else:
                        ins = V.scalar_tensor_tensor(mask[:, h, :], slots[:, 0:E], idx, mask[:, h, :],
                                                     ALU.is_equal, ALU.add)
                    if j < TOPK - 1:
                        run(ins)
                    else:
                        ins.then_inc(s["mask_done"], 1)
                join()
            dve.wait_ge(s["mask_done"], 2)
            dve.wait_ge(s["expd"], 2)
            run(V.tensor_tensor(em, ex, mask, ALU.mult))
            join()
            run(V.tensor_reduce(st[:, 6:8], em, AX, ALU.add))
            join()
            run(V.reciprocal(st[:, 6:8], st[:, 6:8]))
            join()
            for h in range(HALVES):
                run(V.tensor_scalar(wtok[:, h, :].rearrange("p (r e) -> p r e", e=E),
                                    em[:, h, :].unsqueeze(1).to_broadcast([P, ROUNDS, E]), st[:, 6 + h:7 + h], None,
                                    ALU.mult))
            p = filled(dve, "pos")
            pos = ps[:, 2 * p, 0:HALVES * E].rearrange("p (a b) -> p a b", a=HALVES)
            run(V.scalar_tensor_tensor(pm, pos, 1.0, mask, ALU.add, ALU.mult))
            run(V.tensor_reduce(st[:, 8:9], ps[:, 2 * p, 2 * E:3 * E], AX, ALU.max))
            run(V.memset(posm[:, :, PCOLS:PCOLS + 1], -1.0))
            V.memset(yslot, 0.0).then_inc(s["y_ready"], 1)
            join()
            for r in range(ROUNDS):
                run(V.tensor_scalar(posm[:, :, r * E:r * E + E], pm, -1.0 - CAP * r, None, ALU.add))
            run(V.tensor_scalar(st[:, 12:12 + ROUNDS], const[:, C_THR:C_THR + ROUNDS], st[:, 8:9], None, ALU.is_lt))
            join()
            run(V.tensor_reduce(st[:, 9:10], st[:, 12:12 + ROUNDS], AX, ALU.add))
            join()
            V.tensor_copy(nextra[:], st[:, 9:10]).then_inc(s["routed"], 1)
            V.memset(scat, 0.0).then_inc(s["scat_ready"], 1)
            dve.wait_ge(s["routed"], 1)

            def pick_tokens(c, inc):
                for h in range(HALVES):
                    last = V.tensor_scalar(pick[:, h, :], slots[:, 0:CAP], posm[:, h, ds(c, 1)], None, ALU.is_equal)
                last.then_inc(s["pick_ready"], 1)

            def gathered():
                return V.tensor_tensor(xg, ps[:, 2, :].rearrange("p (a b) -> p a b", a=KC),
                                       colA[:, A_FFN:A_FFN + KC].unsqueeze(2).to_broadcast([P, KC, CAP]), ALU.mult)

            pick_tokens(0, 1)
            dve.wait_ge(s["gather_done"], 1)
            gathered().then_inc(s["xg_ready"], 1)
            extra = dve.value_load(nextra[0:1, 0:1], min_val=0, max_val=ROUNDS - 1)

            def add_scattered(n, h):
                dve.wait_ge(s["sc_ready"], n + 1)
                dve.wait_ge(s["sc_used"], n + FIRST)
                V.tensor_tensor(X[:, h, :], X[:, h, :], flat(3), ALU.add).then_inc(s["sc_used"], 1)

            with dve.Fori(0, extra * E + E) as i:
                dve.wait_ge(s["down_done"], i + FIRST)
                V.tensor_copy(esel[0:E, :], const[0:E, ds(i + C_SEL, 1)].to_broadcast([E, CAP])
                              ).then_inc(s["esel_ready"], 1)
                dve.wait_ge(s["scatT_done"], i + FIRST)
                for h in range(HALVES):
                    last = V.tensor_scalar(pickw[:, h, :], slots, posm[:, h, ds(i, 1)], wtok[:, h, ds(i, 1)],
                                           ALU.is_equal, ALU.mult)
                last.then_inc(s["pickw_ready"], 1)
                dve.wait_ge(s["gather_done"], i + 1)
                pick_tokens(i + 1, 1)
                add_scattered(i * 2, 0)
                dve.wait_ge(s["gu_ready"], i + 1)
                V.tensor_scalar(glu, ps[:, 0, :], LIMIT, None, ALU.min).then_inc(s["g_ready"], 1)
                V.tensor_scalar(upc, ps[:, 1, :], LIMIT, -LIMIT, ALU.min, ALU.max).then_inc(s["gu_used"], 1)
                dve.wait_ge(s["g_ready"], i + 1)
                dve.wait_ge(s["gu_used"], i + (1 + FIRST))
                V.scalar_tensor_tensor(upc, upc, 1.0, glu, ALU.add, ALU.mult).then_inc(s["mid_ready"], 1)
                dve.wait_ge(s["mid_ready"], i + 1)
                dve.wait_ge(s["sig_ready"], i + 1)
                V.tensor_tensor(hid, upc, sig, ALU.mult).then_inc(s["hid_ready"], 1)
                dve.wait_ge(s["gather_done"], i + 2)
                gathered().then_inc(s["xg_ready"], 1)
                add_scattered(i * 2 + 1, 1)
            for h in range(HALVES):
                add_scattered(extra * (2 * E) + (2 * E + h), h)

            def w_split(m, l=None):
                dve.wait_ge(s["w_highs"], m + 1 if l is None else l * PER_LAYER + (m + 1))
                V.tensor_tensor(slot3(m + 1, w_low), slot3(m + 1), high_of(m).bitcast(fp32), ALU.subtract
                                ).then_inc(s["w_lows"], 1)

            def x_split(j, n, l=0):
                dve.wait_ge(s["x_highs"], l + n)
                part = slice(4 * j, 4 * j + 4)
                V.tensor_tensor(HT_r[:, part, :], HT[:, part, :], xT_r[0][:, part, :].bitcast(fp32), ALU.subtract
                                ).then_inc(s["x_lows"], 1)

            x_split(0, 1)
            x_split(1, 2)
            w_split(0)
            w_split(1)
            dve.wait_ge(s["ple_sums"], 2)
            V.tensor_scalar(st[:, 0:2], st[:, 0:2], 1.0 / D, EPS, ALU.mult, ALU.add).then_inc(s["pow_in"], 1)
            power()
            assert powers[0] == NORMS
            w_split(2)
            w_split(3)
            T1h = T1.rearrange("p (a b) -> p a b", a=HALVES)
            for g in range(2):
                moved3_(dve, f"g{g}")
                p = filled3(dve, f"pp{g}")
                V.tensor_tensor(T1h, SG.rearrange("p (a b) -> p a b", a=HALVES), pair(p), ALU.mult
                                ).then_inc(s["l_tmp"], 1)
                dve.wait_ge(s["l_tmp"], g + 1)
                part = X[:, :, g * 512:g * 512 + 512]
                ins = V.tensor_tensor(part, part, T1h, ALU.add)
                if g:
                    ins.then_inc(s["x_ready"], 1)
                else:
                    run(ins)
                    join()
            mod_columns(1, filled3(dve, "ada1"), moved3, 1)
            P0 = powers[0]

            with dve.Fori(0, LAYERS) as l:
                nl = [0]

                def lrun(ins):
                    nl[0] += 1
                    ins.then_inc(s["l_step"], 1)

                def ljoin():
                    dve.wait_ge(s["l_step"], l * LSTEPS + nl[0])

                def lfilled(name):
                    return filledL(dve, l, name)

                def lmoved(name):
                    return movedL_(dve, l, name)

                def y_split(c):
                    y, (high, low) = yT3[:, c:c + 4, :], [a[:, c:c + 4, :] for a in yT_r]
                    lrun(V.tensor_copy(high, y))
                    ljoin()
                    V.tensor_tensor(low, y, high.bitcast(fp32), ALU.subtract).then_inc(s["y_lows"], 1)

                w_split(4, l)
                dve.wait_ge(s["l_sums"], l * 2 + 2)
                V.tensor_scalar(st[:, 0:2], st[:, 0:2], 1.0 / D, EPS, ALU.mult, ALU.add).then_inc(s["pow_in"], 1)
                dve.wait_ge(s["pow_out"], l * 2 + (P0 + 1))
                for h in range(HALVES):
                    V.tensor_scalar(HN[:, h, :], X[:, h, :], st[:, h:h + 1], None, ALU.mult).then_inc(s["l_hn"], 1)
                w_split(5, l)
                p = lfilled("hT1")
                for k in range(4):
                    last = V.tensor_scalar(HT[:, 4 + k, :], flat(p, S, k * S), cols(mods_f, 12 + k, l * 24),
                                           cols(mods_f, 4 + k, l * 24), ALU.mult, ALU.add)
                last.then_inc(movedL[p], 1)
                lmoved("hT1")
                lrun(V.tensor_copy(xT_r[0][:, 4:8, :], HT[:, 4:8, :]))
                x_split(0, 3, l)
                ljoin()
                V.tensor_tensor(HT_r[:, 4:8, :], HT[:, 4:8, :], xT_r[0][:, 4:8, :].bitcast(fp32), ALU.subtract
                                ).then_inc(s["x_lows"], 1)
                for m in (6, 7, 8, 9):
                    w_split(m, l)
                lmoved("up")
                dve.wait_ge(s["pads_set"], 4)

                def shifted(a, g0, by):
                    return a[:, g0:4, PAD - by:W3 - by]
                for dst, src, g0, by in ((WA, U, 0, 1), (WB, WA, 1, 2), (WA, WB, 2, 4), (WB, WA, 3, 8)):
                    lrun(V.tensor_tensor(shifted(dst, g0, 0), shifted(src, g0, 0), shifted(src, g0, by), ALU.add))
                    ljoin()
                pl4 = PL.rearrange("p (a b) -> p a b", a=4)
                iv4 = invw.rearrange("p (a b) -> p a b", a=4)
                dve.wait_ge(s["inv_in"], 16)
                for g in range(4):
                    lrun(V.tensor_tensor(pl4[:, g, :], (WA if g % 2 == 0 else WB)[:, g, PAD:W3], iv4[:, g, :], ALU.mult))
                ljoin()
                V.tensor_tensor(pl4, pl4, U[:, :, PAD:W3], ALU.subtract).then_inc(s["l_pooled"], 1)
                gp = mods_f[:, ds(l * 24 + 16, KC)].rearrange("p (a b) -> p a b", b=2)
                V.tensor_tensor(diag.rearrange("p a (b c) -> p a b c", b=2),
                                ident.unsqueeze(1).unsqueeze(1).to_broadcast([P, 4, 2, P]),
                                gp.unsqueeze(3).to_broadcast([P, 4, 2, P]), ALU.mult).then_inc(s["l_diag"], 1)
                p = lfilled("gp")
                dve.wait_ge(s["l_gp_sig"], l + 1)
                V.tensor_tensor(T1, SG, flat(p), ALU.mult).then_inc(movedL[p], 1)
                lmoved("gp")
                w_split(10, l)
                w_split(11, l)
                p = lfilled("mix")
                for g in range(4):
                    last = V.scalar_tensor_tensor(yT3[:, 4 + g, :], flat(p, S, g * S), cols(colA, A_PSC + g, l * 4),
                                                  T1[:, g * S:g * S + S], ALU.mult, ALU.mult)
                last.then_inc(movedL[p], 1)
                lmoved("mix")
                y_split(4)
                w_split(12, l)
                w_split(13, l)
                lmoved("ua")
                p = lfilled("ca")
                V.tensor_tensor(Z[:, :, 2:S + 2], flat(p).rearrange("p (a b) -> p a b", a=4),
                                UA.rearrange("p (a b) -> p a b", a=4), ALU.mult).then_inc(movedL[p], 1)
                lmoved("ca")
                for k in (2, 1, 0):
                    for c in range(4):
                        w = cols(colA, A_CONV + k * 4 + c, l * 12)
                        z = Z[:, c, k:k + S]
                        if k == 2:
                            lrun(V.tensor_scalar(conv[:, c, :], z, w, None, ALU.mult))
                        else:
                            lrun(V.scalar_tensor_tensor(conv[:, c, :], z, w, conv[:, c, :], ALU.mult, ALU.add))
                    ljoin()
                w_split(14, l)
                w_split(15, l)
                p = lfilled("ba")
                V.tensor_tensor(conv, conv, flat(p).rearrange("p (a b) -> p a b", a=4), ALU.mult
                                ).then_inc(movedL[p], 1)
                lmoved("ba")
                for m in (16, 17, 18, 19):
                    w_split(m, l)
                p = lfilled("ga")
                dve.wait_ge(s["l_ga_sig"], l + 1)
                V.tensor_tensor(T1, SG, flat(p), ALU.mult).then_inc(movedL[p], 1)
                lmoved("ga")
                V.tensor_tensor(yT3[:, 0:4, :], conv, T1.rearrange("p (a b) -> p a b", a=4), ALU.mult
                                ).then_inc(s["l_conv"], 1)
                dve.wait_ge(s["l_conv"], l + 1)
                y_split(0)
                dve.wait_ge(s["l_ysum"], l * 4 + 4)
                lrun(V.tensor_reduce(st[:, 0:2], st[:, 8:12].rearrange("p (a b) -> p a b", a=2), AX, ALU.add))
                ljoin()
                V.tensor_scalar(st[:, 0:2], st[:, 0:2], 1.0 / D, EPS, ALU.mult, ALU.add).then_inc(s["pow_in"], 1)
                dve.wait_ge(s["pow_out"], l * 2 + (P0 + 2))
                lmoved("gpb")
                T1h = T1.rearrange("p (a b) -> p a b", a=HALVES)
                for g in range(2):
                    p = UL[f"y{g}"][0]
                    for h in range(HALVES):
                        ins = V.scalar_tensor_tensor(T1h[:, h, :], ps[:, 2 * p + h, :], st[:, h:h + 1],
                                                     UA[:, g * 512:g * 512 + 512], ALU.mult, ALU.mult)
                        if h:
                            ins.then_inc(movedL[p], 1)
                    lmoved(f"y{g}")
                    part = X[:, :, g * 512:g * 512 + 512]
                    ins = V.tensor_tensor(part, part, T1h, ALU.add)
                    if g:
                        ins.then_inc(s["x_ready"], 1)
                    else:
                        lrun(ins)
                        ljoin()
                assert nl[0] == LSTEPS

        @block.tensor
        def _(pe):
            def chunk(n):
                pe.wait_ge(ring1[n % SLOTS1], 16 * (n // SLOTS1 + 1))

            def features(p, src, n=4, w=P):
                for k in range(n):
                    for h in range(HALVES):
                        last = T.transpose(flat(p, P, k * S + h * P)[0:w], src(k, h), ident)
                return last

            pe.wait_ge(s["const_in"], 16)
            pe.wait_ge(s["vec_in"], 16 * 11)
            p = free(pe, "vec")
            T.transpose(ps[:, 2 * p, 0:NA], vec_rows[0:NA, 0, :], ident[0:NA, 0:NA])
            T.transpose(ps[:, 2 * p + 1, 0:NB], vec_rows[0:NB, 1, :], ident[0:NB, 0:NB]).then_inc(full1[p], 1)
            pe.wait_ge(s["hn_done"], 2)
            for j in range(2):
                p = free(pe, f"hT{j}")
                features(p, lambda k, h: HN[:, h, (4 * j + k) * P:(4 * j + k + 1) * P]).then_inc(full1[p], 1)

            def project(gi, kh, halves=(0, 1)):
                name, n, c = GROUP1[gi], col_groups[gi][1], 2 * gi + kh
                chunk(c)
                moved(pe, f"hT{kh}")
                p = free(pe, name)
                for h in halves:
                    for k in range(4):
                        last = T.matmul(ps[:, 2 * p + h, 0:n], HT[:, 4 * kh + k, h * P:h * P + P],
                                        slot1(c, 4, n)[:, k, :], start=kh + k == 0, stop=4 * kh + k == KC - 1)
                if halves[-1]:
                    last.then_inc(s["chunk_used1"], 1)

            def ada_sums(l, p, full):
                for hf in range(2):
                    pe.wait_ge(s[f"used_ada{hf}"], (l + 1) * KC + FIRST)
                for c in range(24):
                    last = T.matmul(ps[:, 2 * p, c:c + 1], acc[l][:, c // 12, c % 12 * P:c % 12 * P + P],
                                    ones[:, 0:1], start=True, stop=True)
                last.then_inc(full[p], 1)

            for gi in range(4):
                for kh in range(2):
                    project(gi, kh)
            moved(pe, "lat")
            p = free(pe, "latT")
            features(p, lambda k, h: lat[:, h, k * P:k * P + P], 3).then_inc(full1[p], 1)
            moved(pe, "latT")
            pe.wait_ge(s["wuq_in"], 16)
            for h in range(HALVES):
                p = free(pe, f"qm{h}")
                for b, (c0, n) in enumerate(((0, 512), (512, 256))):
                    for k in range(2):
                        last = T.matmul(ps[:, 2 * p + b, 0:n], latT[k][:, h * P:h * P + P], wuq[:, k, c0:c0 + n],
                                        start=k == 0, stop=k == 1)
                last.then_inc(full1[p], 1)
            pe.wait_ge(s["wukv_in"], 16)
            for h in range(HALVES):
                p = free(pe, f"kv{h}")
                for b in range(2):
                    last = T.matmul(ps[:, 2 * p + b, :], latT[2][:, h * P:h * P + P], wukv[:, b * 512:b * 512 + 512],
                                    start=True, stop=True)
                last.then_inc(full1[p], 1)

            for gi in (4, 5):
                for kh in range(2):
                    project(gi, kh)
            for name, ready, x in (("qTa", "q_ready", moba[0]), ("kTa", "k_ready", moba[1])):
                pe.wait_ge(s[ready], 1)
                p = free(pe, name)
                features(p, lambda k, h: x[:, h, k * P:k * P + P]).then_inc(full1[p], 1)

            def scores(h):
                bank = 2 * (h % 2)
                if h < HEADS:
                    q, k = [a[64 * (h % 2):64 * (h % 2) + HD, h // 2, :] for a in (qTa, kTa)]
                else:
                    q, k = qTb[0:QK, h - HEADS, :], kTb[0:QK, h - HEADS, :]
                if h >= 2:
                    pe.wait_ge(s["s_free"], h - 1)
                T.matmul(ps[:, bank, 0:P], q[:, 0:P], k[:, 0:P], start=True, stop=True)
                T.matmul(ps[:, bank, P:3 * P], q[:, P:S], k, start=True, stop=True).then_inc(s["s_full"], 1)

            def transpose_probs(h):
                bank = 2 * (h % 2) + 1
                pe.wait_ge(s["prob_done"], h + 1)
                if h >= 2:
                    pe.wait_ge(s["t_free"], h - 1)
                for b in range(3):
                    last = T.transpose(ps[:, bank, b * P:b * P + P], prob[:, h % 2, b * P:b * P + P], ident)
                last.then_inc(s["t_full"], 1)

            def weigh_values(h):
                c = h % HEADS * HD

                def v(half):
                    if h < HEADS:
                        return moba[2][:, half, c:c + HD]
                    return kv[:, half, (h - HEADS) * (NOPE + VD) + NOPE:(h - HEADS + 1) * (NOPE + VD)]
                pt = probT[:, h % 2, :]
                pe.wait_ge(s["t_free"], h + 1)
                T.matmul(ps[:, 6, c:c + HD], pt[:, 0:P], v(0), start=True, stop=True)
                T.matmul(ps[:, 7, c:c + HD], pt[:, P:2 * P], v(0), start=True, stop=False)
                T.matmul(ps[:, 7, c:c + HD], pt[:, 2 * P:3 * P], v(1), start=False, stop=True
                         ).then_inc(s["pv_done"], 1)

            for name in ("qTa", "kTa", "ga0"):
                moved(pe, name)
            for h in range(HEADS + 2):
                if h < HEADS:
                    scores(h)
                    project(6 + h // 4, h // 2 % 2, (h % 2,))
                if 1 <= h <= HEADS:
                    transpose_probs(h - 1)
                if h >= 2:
                    weigh_values(h - 2)
            pe.wait_ge(s["t_free"], HEADS)
            pe.wait_ge(s["s_free"], HEADS)
            for tag, ready, x in (("qTb", "mlaq_ready", qm), ("kTb", "mlak_ready", km)):
                pe.wait_ge(s[ready], 1)
                for j in range(2):
                    p = free(pe, f"{tag}{j}")
                    features(p, lambda k, h: x[:, h, (4 * j + k) * QK:(4 * j + k + 1) * QK], w=QK
                             ).then_inc(full1[p], 1)
            for name in ("qTb0", "qTb1", "kTb0", "kTb1"):
                moved(pe, name)
            for h in range(HEADS, 2 * HEADS + 2):
                if h < 2 * HEADS:
                    scores(h)
                if HEADS + 1 <= h <= 2 * HEADS:
                    transpose_probs(h - 1)
                if h >= HEADS + 2:
                    if h == HEADS + 2:
                        pe.wait_ge(s["y_done"], 1)
                    weigh_values(h - 2)
                if h == 2 * HEADS:
                    ada_sums(0, free(pe, "ada0"), full1)

            for br, name in enumerate(("yTa", "yTb")):
                pe.wait_ge(s["y_done"], br + 1)
                p = free(pe, name)
                if br:
                    pe.wait_ge(s["t_free"], 2 * HEADS)
                features(p, lambda k, h: HN[:, br, h * 512 + k * P:h * 512 + k * P + P]).then_inc(full1[p], 1)
            c = 2 * len(GROUP1)
            for g in range(2):
                for br, name in enumerate(("A", "B")):
                    chunk(c)
                    moved(pe, "yTb" if br else "yTa")
                    p = free(pe, f"{name}{g}")
                    for h in range(HALVES):
                        for k in range(4):
                            last = T.matmul(ps[:, 2 * p + h, :], HT[:, 4 * br + k, h * P:h * P + P],
                                            slot1(c, 4, 512)[:, k, :], start=k == 0, stop=k == 3)
                    last.then_inc(s["chunk_used1"], 1)
                    c += 1
            for j in range(2):
                pe.wait_ge(s["merged_done"], j + 1)
                p = free(pe, f"mT{j}")
                features(p, lambda k, h: merged[:, h, (4 * j + k) * P:(4 * j + k + 1) * P]).then_inc(full1[p], 1)
            for g in range(2):
                for kh in range(2):
                    chunk(c)
                    moved(pe, f"mT{kh}")
                    p = free(pe, f"o{g}")
                    for h in range(HALVES):
                        for k in range(4):
                            last = T.matmul(ps[:, 2 * p + h, :], mT[:, 4 * kh + k, h * P:h * P + P],
                                            slot1(c, 4, 512)[:, k, :], start=kh + k == 0, stop=4 * kh + k == KC - 1)
                    last.then_inc(s["chunk_used1"], 1)
                    c += 1
            for g in range(2):
                moved(pe, f"o{g}")
            for j in range(2):
                p = free(pe, f"fT{j}")
                features(p, lambda k, h: X[:, h, (4 * j + k) * P:(4 * j + k + 1) * P]).then_inc(full1[p], 1)
            moved(pe, "fT0")
            moved(pe, "fT1")
            pe.wait_ge(s["wr_in"], 16)
            p = free(pe, "rt")
            for h in range(HALVES):
                for k in range(KC):
                    last = T.matmul(ps[:, 2 * p, h * E:h * E + E], HT[:, k, h * P:h * P + P], wr[:, k, :],
                                    start=k == 0, stop=k == KC - 1)
            last.then_inc(full1[p], 1)
            pe.wait_ge(s["mask_done"], 2)
            p = free(pe, "pos")
            T.matmul(ps[:, 2 * p, 0:E], before, mask[:, 0, :], start=True, stop=True)
            T.matmul(ps[:, 2 * p, E:2 * E], ones, mask[:, 0, :], start=True, stop=False)
            T.matmul(ps[:, 2 * p, E:2 * E], before, mask[:, 1, :], start=False, stop=True)
            T.matmul(ps[:, 2 * p, 2 * E:3 * E], ones, mask[:, 0, :], start=True, stop=False)
            T.matmul(ps[:, 2 * p, 2 * E:3 * E], ones, mask[:, 1, :], start=False, stop=True).then_inc(full1[p], 1)

            def gather():
                for k in range(KC):
                    for h in range(HALVES):
                        last = T.matmul(ps[:, 2, k * CAP:k * CAP + CAP], HN[:, h, k * P:k * P + P], pick[:, h, :],
                                        start=h == 0, stop=h == HALVES - 1)
                last.then_inc(s["gather_done"], 1)

            def scatter(h):
                for g in range(2):
                    last = T.matmul(ps[:, 6 + g, :], scat[64 * g:64 * g + CAP, h, :], yslot[64 * g:64 * g + CAP, :],
                                    start=True, stop=True)
                last.then_inc(s["sc_ready"], 1)

            def side_by_side(bank, lhsT, w, start, stop):
                for g in range(2):
                    last = T.matmul(ps[64 * g:64 * g + CAP, bank, :], lhsT, w(g), start=start, stop=stop)
                return last

            pe.wait_ge(s["hn2_done"], 2)
            pe.wait_ge(s["pick_ready"], 1)
            gather()
            pe.wait_ge(s["bias_in"], 32)
            extra = pe.value_load(nextra[0:1, 0:1], min_val=0, max_val=ROUNDS - 1)
            with pe.Fori(0, extra * E + E) as i:
                pe.wait_ge(s["xg_ready"], i + 1)
                pe.wait_ge(s["gu_used"], i + FIRST)
                for k in range(KC):
                    pe.wait_ge(ring2[k], i * 16 + 16)
                    side_by_side(0, xg[:, k, :], lambda g: ring[:, k, g * 512:g * 512 + 512], k == 0, False)
                    side_by_side(1, xg[:, k, :], lambda g: ring[:, k, F + g * 512:F + g * 512 + 512], k == 0, False
                                 ).then_inc(s["chunk_used2"], 1)
                    if k == 2:
                        pe.wait_ge(s["y_ready"], i + FIRST)
                        pe.wait_ge(s["scat_ready"], i + FIRST)
                        pe.wait_ge(s["sc_used"], i * 2 + FIRST)
                        scatter(0)
                pe.wait_ge(s["esel_ready"], i + 1)
                side_by_side(0, esel[0:E, :], lambda g: bias[0:E, g * 512:g * 512 + 512], False, True)
                side_by_side(1, esel[0:E, :], lambda g: bias[0:E, F + g * 512:F + g * 512 + 512], False, True
                             ).then_inc(s["gu_ready"], 1)
                pe.wait_ge(s["pick_ready"], i + 2)
                gather()
                pe.wait_ge(s["pickw_ready"], i + 1)
                for h in range(HALVES):
                    last = T.transpose(ps[:, 4, h * P:h * P + P], pickw[:, h, :], ident)
                last.then_inc(s["scatT_done"], 1)
                pe.wait_ge(s["hid_ready"], i + 1)
                for c in range(4):
                    last = T.transpose(ps[:, 3, c * P:c * P + P], hid[:, c * P:c * P + P], ident)
                last.then_inc(s["hidT_full"], 1)
                pe.wait_ge(s["sc_used"], i * 2 + (1 + FIRST))
                scatter(1)
                pe.wait_ge(s["hidT_ready"], i + 1)
                pe.wait_ge(s["y_ready"], i + FIRST)
                for c in range(KC):
                    if c % 2 == 0:
                        pe.wait_ge(ring2[KC + c // 2], i * 16 + 16)
                    w = slot(KC + c // 2, 2, D)[:, c % 2, :]
                    at = c % 4 * P + c // 4 * CAP
                    last = side_by_side(5, hidT[:, at:at + CAP], lambda g: w[:, g * 512:g * 512 + 512], c == 0, False)
                    if c % 2:
                        last.then_inc(s["chunk_used2"], 1)
                side_by_side(5, esel[0:E, :], lambda g: bias[0:E, 2 * F + g * 512:2 * F + g * 512 + 512], False, True
                             ).then_inc(s["down_done"], 1)
            pe.wait_ge(s["y_ready"], extra * E + (E + FIRST))
            for h in range(HALVES):
                pe.wait_ge(s["sc_used"], extra * (2 * E) + (2 * E + h + FIRST))
                scatter(h)

            pe.wait_ge(s["p_in"], 16)
            p = U3["pT"][0]
            features(p, lambda k, h: pin[:, h, k * P:k * P + P], 2).then_inc(full3[p], 1)
            moved3_(pe, "pT")
            pe.wait_ge(ring3[0], 16)
            for g in range(2):
                p = U3[f"pp{g}"][0]
                for h in range(HALVES):
                    for k in range(2):
                        last = T.matmul(ps[:, 2 * p + h, :], pT[:, k, h * P:h * P + P],
                                        slot(0, 2, D)[:, k, g * 512:g * 512 + 512], start=k == 0, stop=k == 1)
            last.then_inc(s["chunk_used3"], 1)
            pe.wait_ge(s["sc_used"], extra * (2 * E) + (2 * E + 2 + FIRST))
            for j in range(2):
                p = U3[f"hT{j}"][0]
                features(p, lambda k, h: X[:, h, (4 * j + k) * P:(4 * j + k + 1) * P]).then_inc(full3[p], 1)
            def terms(out, lhs, rhs, first, last):
                T.matmul(out, lhs[0], rhs[0], start=first, stop=False)
                T.matmul(out, lhs[0], rhs[1], start=False, stop=False)
                return T.matmul(out, lhs[1], rhs[0], start=False, stop=last)

            pe.wait_ge(s["x_lows"], 2)
            for g in range(2):
                p = U3[f"g{g}"][0]
                for kh in range(2):
                    m = 2 * g + kh
                    pe.wait_ge(s["w_lows"], m + 1)
                    w = chunk_parts(m)
                    for h in range(HALVES):
                        for k in range(4):
                            last = terms(ps[:, 2 * p + h, :], [x[:, 4 * kh + k, h * P:h * P + P] for x in xT_r],
                                         [a[:, k, :] for a in w], kh + k == 0, 4 * kh + k == KC - 1)
                    last.then_inc(s["chunk_used3"], 1)

            pe.wait_ge(s["l_tmp"], 1)
            ada_sums(1, U3["ada1"][0], full3)

            with pe.Fori(0, LAYERS) as l:
                def lfree(name):
                    p, _, moves, _ = UL[name]
                    pe.wait_ge(movedL[p], l * LM[p] + (moves + FIRST))
                    return p

                pe.wait_ge(s["l_hn"], l * 2 + 2)
                for j in range(2):
                    p = lfree(f"hT{j}")
                    features(p, lambda k, h: HN[:, h, (4 * j + k) * P:(4 * j + k + 1) * P]).then_inc(fullL[p], 1)
                pe.wait_ge(s["x_lows"], l * 2 + 4)

                def group(i):
                    p = lfree(GROUPL[i][0])
                    m = PRE3 - 1 + 2 * i
                    pe.wait_ge(s["w_lows"], l * PER_LAYER + (m + 2))
                    w = [chunk_parts(m), chunk_parts(m + 1)]
                    for c in range(4):
                        for k in range(KC):
                            last = terms(flat(p, S, c * S), [a[:, k % 4, c * P:c * P + P] for a in w[k // 4]],
                                         [x[:, k, :] for x in xT_r], k == 0, k == KC - 1)
                            if c == 3 and k % 4 == 3:
                                last.then_inc(s["chunk_used3"], 1)

                for i in range(3):
                    group(i)
                p = lfree("mix")
                pe.wait_ge(s["l_pooled"], l + 1)
                pe.wait_ge(s["wpool_in"], l * 16 + 16)
                for g in range(4):
                    last = T.matmul(flat(p, S, g * S), wpool[:, g, :], PL[:, g * S:g * S + S], start=True, stop=True)
                last.then_inc(fullL[p], 1)
                for i in range(3, 6):
                    group(i)
                p = lfree("gpb")
                pe.wait_ge(s["l_diag"], l + 1)
                for b in range(2):
                    last = T.matmul(ps[:, 2 * p + b, :], ones, diag[:, 2 * b:2 * b + 2, :], start=True, stop=True)
                last.then_inc(fullL[p], 1)
                m = PRE3 - 1 + 2 * len(GROUPL)
                for part in range(2):
                    pe.wait_ge(s["y_lows"], l * 2 + (part + 1))
                    for g in range(2):
                        p = UL[f"y{g}"][0]
                        if not part:
                            lfree(f"y{g}")
                        pe.wait_ge(s["w_lows"], l * PER_LAYER + (m + 1))
                        w = chunk_parts(m)
                        for h in range(HALVES):
                            for k in range(4):
                                c = 4 - 4 * part + k
                                last = terms(ps[:, 2 * p + h, :], [y[:, c, h * P:h * P + P] for y in yT_r],
                                             [a[:, k, :] for a in w], part + k == 0, part == 1 and k == 3)
                        last.then_inc(s["chunk_used3"], 1)
                        m += 1


_INS = ["x", "p", "g_mix", "w_in", "moba_q_norm", "moba_k_norm", "mla_q_lat_norm", "w_uq", "mla_kv_lat_norm", "w_ukv",
        "mla_q_norm", "mla_k_norm", "w_branch_a", "w_branch_b", "w_out", "g_ffn", "w_router", "b_router", "w_gate_up",
        "b_gate_up", "w_down", "b_down", "g_ple", "w_ple_gate", "w_ple_proj", "c_2", "w_ada_2", "b_ada_2", "g_pre_2",
        "w_in_2", "w_conv_2", "w_pool_2", "pool_scale_2", "w_out_2", "g_post_2"]


def kernel(**inputs):
    import numpy as _np
    import concourse.bacc as _bacc
    from concourse import mybir as _mybir
    from concourse.bass_utils import run_bass_kernel_spmd as _run

    nc = _bacc.Bacc("TRN2", target_bir_lowering=False, num_devices=1)
    arrays, t = {}, {}
    consts, inv = shape_constants()
    for name, a in [(n, inputs[n]) for n in _INS] + [("consts", consts), ("inv_windows", inv)]:
        a = _np.ascontiguousarray(a)
        arrays[f"in_{name}_dram"] = a
        t[name] = nc.dram_tensor(f"in_{name}_dram", a.shape, _mybir.dt.from_np(a.dtype), kind="ExternalInput").ap()
    out = nc.dram_tensor("out_dram", (1, S, D), _mybir.dt.float32, kind="ExternalOutput").ap()
    build(nc, t, out)
    r = _run(nc, [arrays], core_ids=[0])
    return r.results[0]["out_dram"]
```
